# Optimizing a Trainium2 kernel written in Bass

```python
import math
import jax, jax.numpy as jnp
from jax import lax
import numpy as np

D_MODEL = 1024
BATCH = 1
SEQ = 512
DEPTH = 2

N_A_LAYERS = DEPTH // 2
N_B_LAYERS = DEPTH - N_A_LAYERS
N_HEADS = 16
HEAD_DIM = 64
N_KV_GROUPS = 4
HEADS_PER_GROUP = N_HEADS // N_KV_GROUPS
D_FF = 4 * D_MODEL
CONV_WIDTH = 3
CMP_BLOCK = 32
CMP_STRIDE = 16
SEL_BLOCK = 64
SEL_TOP_N = 16
WINDOW = 512
PHI_HIDDEN = 256
N_BUCKETS = 32
MAX_DISTANCE = 128
Q_BLOCK = 128
EPS = 1e-6
NEG_INF = -1e30
FORCED_SCORE = 1e9


def rms_norm(x, g):
    xf = x.astype(jnp.float32)
    y = xf * lax.rsqrt(jnp.mean(xf * xf, axis=-1, keepdims=True) + EPS)
    return (y * g.astype(jnp.float32)).astype(x.dtype)

def t5_bucket(dist):
    dist = jnp.maximum(dist, 0)
    max_exact = N_BUCKETS // 2
    logd = jnp.log(jnp.maximum(dist, 1).astype(jnp.float32) / max_exact)
    large = max_exact + (logd / math.log(MAX_DISTANCE / max_exact)
                         * (N_BUCKETS - max_exact)).astype(jnp.int32)
    large = jnp.minimum(large, N_BUCKETS - 1)
    return jnp.where(dist < max_exact, dist, large)

def short_conv_mixer(h, w_in, conv_w, w_out):
    S = h.shape[1]
    b_gate, c_gate, u = jnp.split(h @ w_in, 3, axis=-1)
    v = c_gate * u
    vp = jnp.pad(v, ((0, 0), (CONV_WIDTH - 1, 0), (0, 0)))
    conv = sum(conv_w[k] * vp[:, k:k + S] for k in range(CONV_WIDTH))
    return (b_gate * conv) @ w_out

def squared_relu_mlp(h, w1, w2):
    return jnp.square(jax.nn.relu(h @ w1)) @ w2

def compress_blocks(t, pe, w1, w2):
    B, S, G, dh = t.shape
    chunks = t.reshape(B, S // CMP_STRIDE, CMP_STRIDE, G, dh)
    blocks = jnp.concatenate([chunks[:, :-1], chunks[:, 1:]], axis=2)
    blocks = blocks + pe[None, None, :, None, :]
    n_cmp = blocks.shape[1]
    flat = jnp.moveaxis(blocks, 2, 3).reshape(B, n_cmp, G, CMP_BLOCK * dh)
    return jax.nn.silu(flat @ w1) @ w2

def nsa_shared_kv(h, w_kv, cmp_pe_k, cmp_pe_v, phi_k_w1, phi_k_w2, phi_v_w1, phi_v_w2):
    B, S, _ = h.shape
    kv = (h @ w_kv).reshape(B, S, 6, N_KV_GROUPS, HEAD_DIM)
    k_raw, v_raw = kv[:, :, 0], kv[:, :, 1]
    k_sel, v_sel = kv[:, :, 2], kv[:, :, 3]
    k_win, v_win = kv[:, :, 4], kv[:, :, 5]
    k_cmp = compress_blocks(k_raw, cmp_pe_k, phi_k_w1, phi_k_w2)
    v_cmp = compress_blocks(v_raw, cmp_pe_v, phi_v_w1, phi_v_w2)
    return (k_cmp, v_cmp, k_sel, v_sel, k_win, v_win)

def nsa_attention(q, gates, k_cmp, v_cmp, k_sel, v_sel, k_win, v_win, rel_bias):
    B, S, G, Hg, dh = q.shape
    n_cmp = k_cmp.shape[1]
    n_selb = S // SEL_BLOCK
    top_n = min(SEL_TOP_N, n_selb)
    n_qb = S // Q_BLOCK
    bias_g = rel_bias.reshape(N_BUCKETS, G, Hg)

    cmp_end = jnp.arange(n_cmp) * CMP_STRIDE + CMP_BLOCK - 1
    ratio = SEL_BLOCK // CMP_STRIDE
    span = CMP_BLOCK // CMP_STRIDE
    offs = (jnp.arange(ratio)[:, None] - jnp.arange(span)[None, :]).reshape(-1)
    map_idx = ratio * jnp.arange(n_selb)[:, None] + offs[None, :]
    map_ok = (map_idx >= 0) & (map_idx < n_cmp)
    map_idx = jnp.clip(map_idx, 0, n_cmp - 1)

    k_sel_bg = jnp.transpose(k_sel.reshape(B, n_selb, SEL_BLOCK, G, dh), (0, 3, 1, 2, 4))
    v_sel_bg = jnp.transpose(v_sel.reshape(B, n_selb, SEL_BLOCK, G, dh), (0, 3, 1, 2, 4))
    k_win_p = jnp.pad(k_win, ((0, 0), (WINDOW, 0), (0, 0), (0, 0)))
    v_win_p = jnp.pad(v_win, ((0, 0), (WINDOW, 0), (0, 0), (0, 0)))
    b_ix = jnp.arange(B)[:, None, None, None]
    g_ix = jnp.arange(G)[None, None, :, None]
    jb = jnp.arange(n_selb)

    def one_block(qb):
        t0 = qb * Q_BLOCK
        qt = lax.dynamic_slice_in_dim(q, t0, Q_BLOCK, axis=1)
        gt = lax.dynamic_slice_in_dim(gates, t0, Q_BLOCK, axis=1)
        pos = t0 + jnp.arange(Q_BLOCK)

        d_c = pos[:, None] - cmp_end[None, :]
        valid_c = d_c >= 0
        bias_c = jnp.transpose(bias_g[t5_bucket(d_c)], (0, 2, 3, 1)).astype(jnp.float32)
        logit_c = jnp.einsum('bqghd,bngd->bqghn', qt, k_cmp).astype(jnp.float32) + bias_c[None]
        logit_c = jnp.where(valid_c[None, :, None, None, :], logit_c, NEG_INF)
        has_any = jnp.any(valid_c, axis=-1).astype(jnp.float32)
        p_c = jax.nn.softmax(logit_c, axis=-1) * has_any[None, :, None, None, None]
        o_c = jnp.einsum('bqghn,bngd->bqghd', p_c.astype(v_cmp.dtype), v_cmp)

        imp = p_c.sum(axis=3)
        imp_s = jnp.sum(jnp.where(map_ok, jnp.take(imp, map_idx, axis=-1), 0.0), axis=-1)
        cb = pos // SEL_BLOCK
        forced = (jb[None, :] == 0) | (jb[None, :] == cb[:, None]) | (jb[None, :] == cb[:, None] - 1)
        future = jb[None, :] > cb[:, None]
        score = jnp.where(forced[None, :, None, :], FORCED_SCORE, imp_s)
        score = jnp.where(future[None, :, None, :], NEG_INF, score)
        top_s, top_idx = lax.top_k(score, top_n)
        blk_ok = top_s > NEG_INF * 0.5

        ks = k_sel_bg[b_ix, g_ix, top_idx].reshape(B, Q_BLOCK, G, top_n * SEL_BLOCK, dh)
        vs = v_sel_bg[b_ix, g_ix, top_idx].reshape(B, Q_BLOCK, G, top_n * SEL_BLOCK, dh)
        kpos = (top_idx[..., None] * SEL_BLOCK + jnp.arange(SEL_BLOCK)).reshape(B, Q_BLOCK, G, -1)
        blk_ok_k = jnp.repeat(blk_ok, SEL_BLOCK, axis=-1)
        d_s = pos[None, :, None, None] - kpos
        valid_s = blk_ok_k & (d_s >= 0)
        bias_s = jnp.transpose(bias_g[t5_bucket(d_s), g_ix], (0, 1, 2, 4, 3)).astype(jnp.float32)
        logit_s = jnp.einsum('bqghd,bqgkd->bqghk', qt, ks).astype(jnp.float32) + bias_s
        logit_s = jnp.where(valid_s[:, :, :, None, :], logit_s, NEG_INF)
        p_s = jax.nn.softmax(logit_s, axis=-1)
        o_s = jnp.einsum('bqghk,bqgkd->bqghd', p_s.astype(vs.dtype), vs)

        kw = lax.dynamic_slice_in_dim(k_win_p, t0, Q_BLOCK + WINDOW, axis=1)
        vw = lax.dynamic_slice_in_dim(v_win_p, t0, Q_BLOCK + WINDOW, axis=1)
        wpos = t0 - WINDOW + jnp.arange(Q_BLOCK + WINDOW)
        d_w = pos[:, None] - wpos[None, :]
        valid_w = (d_w >= 0) & (d_w < WINDOW) & (wpos[None, :] >= 0)
        bias_w = jnp.transpose(bias_g[t5_bucket(d_w)], (0, 2, 3, 1)).astype(jnp.float32)
        logit_w = jnp.einsum('bqghd,bkgd->bqghk', qt, kw).astype(jnp.float32) + bias_w[None]
        logit_w = jnp.where(valid_w[None, :, None, None, :], logit_w, NEG_INF)
        p_w = jax.nn.softmax(logit_w, axis=-1)
        o_w = jnp.einsum('bqghk,bkgd->bqghd', p_w.astype(vw.dtype), vw)

        o = gt[..., 0:1] * o_c + gt[..., 1:2] * o_s + gt[..., 2:3] * o_w
        return o.astype(q.dtype)

    o = lax.map(one_block, jnp.arange(n_qb))
    return jnp.moveaxis(o, 0, 1).reshape(B, S, G, Hg, dh)

def nsa_mixer(h, w_qg, w_o, shared, rel_bias):
    B, S, _ = h.shape
    qg = h @ w_qg
    q = qg[..., :N_HEADS * HEAD_DIM].reshape(B, S, N_KV_GROUPS, HEADS_PER_GROUP, HEAD_DIM)
    q = q * (HEAD_DIM ** -0.5)
    gates = jax.nn.sigmoid(qg[..., N_HEADS * HEAD_DIM:].astype(jnp.float32))
    gates = gates.reshape(B, S, N_KV_GROUPS, HEADS_PER_GROUP, 3)
    k_cmp, v_cmp, k_sel, v_sel, k_win, v_win = shared
    o = nsa_attention(q, gates, k_cmp, v_cmp, k_sel, v_sel, k_win, v_win, rel_bias)
    return o.reshape(B, S, N_HEADS * HEAD_DIM) @ w_o

def first_inputs(seed: int = 0) -> dict:
    key = jax.random.key(seed)
    ks = jax.random.split(key, 22)
    f32 = jnp.float32
    D, H, G, dh = D_MODEL, N_HEADS, N_KV_GROUPS, HEAD_DIM

    def nrm(k, shape, scale):
        return jax.random.normal(k, shape, f32) * scale

    return {
        "x": nrm(ks[0], (BATCH, SEQ, D), 1.0),
        "rel_bias": nrm(ks[1], (N_BUCKETS, H), 0.5),
        "norm_mix": 1.0 + nrm(ks[2], (DEPTH, D), 0.1),
        "norm_mlp": 1.0 + nrm(ks[3], (DEPTH, D), 0.1),
        "mlp_w1": nrm(ks[4], (DEPTH, D, D_FF), D ** -0.5),
        "mlp_w2": nrm(ks[5], (DEPTH, D_FF, D), 0.5 * D_FF ** -0.5),
        "a_w_in": nrm(ks[6], (N_A_LAYERS, D, 3 * D), D ** -0.5),
        "a_conv_w": nrm(ks[7], (N_A_LAYERS, CONV_WIDTH, D), CONV_WIDTH ** -0.5),
        "a_w_out": nrm(ks[8], (N_A_LAYERS, D, D), D ** -0.5),
        "kv_norm": 1.0 + nrm(ks[9], (D,), 0.1),
        "w_kv": nrm(ks[10], (D, 6 * G * dh), D ** -0.5),
        "cmp_pe_k": nrm(ks[11], (CMP_BLOCK, dh), 0.1),
        "cmp_pe_v": nrm(ks[12], (CMP_BLOCK, dh), 0.1),
        "phi_k_w1": nrm(ks[13], (CMP_BLOCK * dh, PHI_HIDDEN), (CMP_BLOCK * dh) ** -0.5),
        "phi_k_w2": nrm(ks[14], (PHI_HIDDEN, dh), PHI_HIDDEN ** -0.5),
        "phi_v_w1": nrm(ks[15], (CMP_BLOCK * dh, PHI_HIDDEN), (CMP_BLOCK * dh) ** -0.5),
        "phi_v_w2": nrm(ks[16], (PHI_HIDDEN, dh), PHI_HIDDEN ** -0.5),
        "b_w_qg": nrm(ks[17], (N_B_LAYERS, D, H * dh + 3 * H), D ** -0.5),
        "b_w_o": nrm(ks[18], (N_B_LAYERS, H * dh, D), (H * dh) ** -0.5),
        "final_norm": 1.0 + nrm(ks[19], (D,), 0.1),
    }

def first_block(x, rel_bias, norm_mix, norm_mlp, mlp_w1, mlp_w2, a_w_in, a_conv_w, a_w_out,
              kv_norm, w_kv, cmp_pe_k, cmp_pe_v, phi_k_w1, phi_k_w2, phi_v_w1, phi_v_w2,
              b_w_qg, b_w_o, final_norm):
    shared = None
    for layer in range(DEPTH):
        h = rms_norm(x, norm_mix[layer])
        if layer < N_A_LAYERS:
            x = x + short_conv_mixer(h, a_w_in[layer], a_conv_w[layer], a_w_out[layer])
        else:
            i = layer - N_A_LAYERS
            x = x + nsa_mixer(h, b_w_qg[i], b_w_o[i], shared, rel_bias)
        x = x + squared_relu_mlp(rms_norm(x, norm_mlp[layer]), mlp_w1[layer], mlp_w2[layer])
        if layer == N_A_LAYERS - 1:
            shared = nsa_shared_kv(rms_norm(x, kv_norm), w_kv, cmp_pe_k, cmp_pe_v,
                                   phi_k_w1, phi_k_w2, phi_v_w1, phi_v_w2)
    return rms_norm(x, final_norm)


DEPTH_2 = 1

N_META = 16
BLOCK = 128
PAD = BLOCK - N_META
NEG = -1e30
SSD_INNER = 2 * D_MODEL
SSD_HEADDIM = 64
SSD_HEADS = SSD_INNER // SSD_HEADDIM
SSD_GROUPS = 4
SSD_HPG = SSD_HEADS // SSD_GROUPS
SSD_STATE = 128
SSD_CONV = 4
SSD_XBC = SSD_INNER + 2 * SSD_GROUPS * SSD_STATE
ATT_HEADS = 16
ATT_KV_HEADS = 2
ATT_HEADDIM = 64
ATT_GQ = ATT_HEADS // ATT_KV_HEADS
WINDOW_2 = 128
ATT_Q = ATT_HEADS * ATT_HEADDIM
ATT_KV = ATT_KV_HEADS * ATT_HEADDIM
REL_BUCKETS = 32
REL_MAX_DIST = 128
D_FF_2 = 2816
FFN_CONV = 3
N_BRANCH = 2
IN_WIDTHS = (SSD_INNER, SSD_XBC, SSD_HEADS, ATT_Q, ATT_KV, ATT_KV, D_MODEL, D_MODEL)
D_IN_PROJ = SSD_INNER + SSD_XBC + SSD_HEADS + ATT_Q + 2 * ATT_KV + N_BRANCH * D_MODEL


def rmsnorm(x, w):
    xf = x.astype(jnp.float32)
    y = xf * lax.rsqrt(jnp.mean(xf * xf, axis=-1, keepdims=True) + EPS)
    return (y * w.astype(jnp.float32)).astype(x.dtype)

def split_cols(t, widths):
    idx, acc = [], 0
    for w in widths[:-1]:
        acc += w
        idx.append(acc)
    return jnp.split(t, idx, axis=-1)

def causal_dwconv(x, w, b):
    k = w.shape[0]
    y = lax.conv_general_dilated(x, w[:, None, :].astype(x.dtype), window_strides=(1,),
                                 padding=[(k - 1, 0)], dimension_numbers=('NWC', 'WIO', 'NWC'),
                                 feature_group_count=x.shape[-1])
    return y + b.astype(x.dtype)

def t5_bucket_2(dist):
    max_exact = REL_BUCKETS // 2
    d = jnp.maximum(dist, 0)
    big = max_exact + (jnp.log(jnp.maximum(d, max_exact).astype(jnp.float32) / max_exact)
                       / math.log(REL_MAX_DIST / max_exact) * (REL_BUCKETS - max_exact)).astype(jnp.int32)
    return jnp.where(d < max_exact, d, jnp.minimum(big, REL_BUCKETS - 1))

def ssd_chunked(x, dt, a, bmat, cmat):
    bsz, lp = x.shape[:2]
    nc = lp // BLOCK
    f32 = jnp.float32
    xc = x.reshape(bsz, nc, BLOCK, SSD_GROUPS, SSD_HPG, SSD_HEADDIM).astype(f32)
    dtc = dt.reshape(bsz, nc, BLOCK, SSD_GROUPS, SSD_HPG)
    bc = bmat.reshape(bsz, nc, BLOCK, SSD_GROUPS, SSD_STATE).astype(f32)
    cc = cmat.reshape(bsz, nc, BLOCK, SSD_GROUPS, SSD_STATE).astype(f32)
    cs = jnp.cumsum(dtc * a.reshape(SSD_GROUPS, SSD_HPG), axis=2)
    xdt = xc * dtc[..., None]
    cs_t = jnp.moveaxis(cs, 2, -1)
    causal = jnp.tril(jnp.ones((BLOCK, BLOCK), dtype=bool))
    lmat = jnp.exp(jnp.where(causal, cs_t[..., :, None] - cs_t[..., None, :], -jnp.inf))
    cb = jnp.einsum('bclgn,bcsgn->bcgls', cc, bc)
    y_diag = jnp.einsum('bcgls,bcgrls,bcsgrp->bclgrp', cb, lmat, xdt)
    decay_states = jnp.exp(cs[:, :, -1:] - cs)
    states = jnp.einsum('bclgn,bclgr,bclgrp->bcgrpn', bc, decay_states, xdt)
    chunk_decay = jnp.exp(cs[:, :, -1])

    def step(hst, inp):
        st, dec = inp
        return dec[..., None, None] * hst + st, hst

    h0 = jnp.zeros((bsz, SSD_GROUPS, SSD_HPG, SSD_HEADDIM, SSD_STATE), f32)
    _, prev = lax.scan(step, h0, (jnp.moveaxis(states, 1, 0), jnp.moveaxis(chunk_decay, 1, 0)))
    prev = jnp.moveaxis(prev, 0, 1)
    y_off = jnp.einsum('bclgn,bcgrpn,bclgr->bclgrp', cc, prev, jnp.exp(cs))
    return (y_diag + y_off).reshape(bsz, lp, SSD_HEADS, SSD_HEADDIM)

def gated_group_rmsnorm(y, z, w):
    g = y * jax.nn.silu(z.astype(jnp.float32))
    gg = g.reshape(g.shape[:-1] + (SSD_GROUPS, SSD_INNER // SSD_GROUPS))
    gg = gg * lax.rsqrt(jnp.mean(gg * gg, axis=-1, keepdims=True) + EPS)
    return gg.reshape(g.shape) * w.astype(jnp.float32)

def swa_sink_attention(q, k, v, rel_bias, sinks):
    bsz, lp = q.shape[:2]
    nb = lp // BLOCK
    f32 = jnp.float32
    scale = ATT_HEADDIM ** -0.5
    qb = q.reshape(bsz, nb, BLOCK, ATT_KV_HEADS, ATT_GQ, ATT_HEADDIM)
    kb = k.reshape(bsz, nb, BLOCK, ATT_KV_HEADS, ATT_HEADDIM)
    vb = v.reshape(bsz, nb, BLOCK, ATT_KV_HEADS, ATT_HEADDIM)

    def with_prev(t):
        prev = jnp.pad(t, ((0, 0), (1, 0), (0, 0), (0, 0), (0, 0)))[:, :-1]
        return jnp.concatenate([prev, t], axis=2)

    kband, vband = with_prev(kb), with_prev(vb)
    pos = jnp.arange(lp, dtype=jnp.int32).reshape(nb, BLOCK)
    k_pos = jnp.concatenate([pos - BLOCK, pos], axis=1)
    dist = pos[:, :, None] - k_pos[:, None, :]
    mask_band = (k_pos[:, None, :] >= BLOCK) & (dist >= 0) & (dist < WINDOW_2)
    bias_band = rel_bias[t5_bucket_2(dist[0])].astype(f32)
    bias_band = jnp.transpose(bias_band, (2, 0, 1)).reshape(ATT_KV_HEADS, ATT_GQ, BLOCK, 2 * BLOCK)
    s_band = jnp.einsum('bnqkgd,bnskd->bnkgqs', qb, kband, preferred_element_type=f32) * scale + bias_band
    s_band = jnp.where(mask_band[None, :, None, None], s_band, NEG)
    meta_pos = PAD + jnp.arange(N_META, dtype=jnp.int32)
    k_meta, v_meta = k[:, PAD:BLOCK], v[:, PAD:BLOCK]
    dist_m = pos[:, :, None] - meta_pos[None, None, :]
    bias_m = rel_bias[t5_bucket_2(dist_m)].astype(f32)
    bias_m = jnp.transpose(bias_m, (0, 3, 1, 2)).reshape(nb, ATT_KV_HEADS, ATT_GQ, BLOCK, N_META)
    s_meta = jnp.einsum('bnqkgd,bmkd->bnkgqm', qb, k_meta, preferred_element_type=f32) * scale + bias_m[None]
    s_meta = jnp.where((dist_m >= 0)[None, :, None, None], s_meta, NEG)
    sink = jnp.broadcast_to(sinks.astype(f32).reshape(1, 1, ATT_KV_HEADS, ATT_GQ, 1, 1),
                            s_meta.shape[:-1] + (1,))
    p = jax.nn.softmax(jnp.concatenate([s_meta, s_band, sink], axis=-1), axis=-1)
    p_meta = p[..., :N_META].astype(v.dtype)
    p_band = p[..., N_META:-1].astype(v.dtype)
    out = (jnp.einsum('bnkgqm,bmkd->bnqkgd', p_meta, v_meta)
           + jnp.einsum('bnkgqs,bnskd->bnqkgd', p_band, vband))
    return out.reshape(bsz, lp, ATT_Q)

def mixer_block(h, valid_f32, norm_w, w_in, conv_w, conv_b, dt_bias, a_log, d_skip, ssd_norm_w,
                w_ssd_branch, w_attn_branch, sinks, rel_bias, gate_b, w_out):
    bsz, lp = h.shape[:2]
    f32 = jnp.float32
    u = rmsnorm(h, norm_w)
    z, xbc, dt_raw, q, k, v, g_ssd, g_att = split_cols(u @ w_in.astype(u.dtype), IN_WIDTHS)
    xbc = jax.nn.silu(causal_dwconv(xbc, conv_w, conv_b))
    xs, bm, cm = split_cols(xbc, (SSD_INNER, SSD_GROUPS * SSD_STATE, SSD_GROUPS * SSD_STATE))
    dt = jax.nn.softplus(dt_raw.astype(f32) + dt_bias.astype(f32)) * valid_f32[None, :, None]
    a = -jnp.exp(a_log.astype(f32))
    xh = xs.reshape(bsz, lp, SSD_HEADS, SSD_HEADDIM)
    y = ssd_chunked(xh, dt, a, bm.reshape(bsz, lp, SSD_GROUPS, SSD_STATE),
                    cm.reshape(bsz, lp, SSD_GROUPS, SSD_STATE))
    y = y + d_skip.astype(f32)[:, None] * xh.astype(f32)
    y = gated_group_rmsnorm(y.reshape(bsz, lp, SSD_INNER), z, ssd_norm_w).astype(h.dtype)
    y_ssd = y @ w_ssd_branch.astype(h.dtype)
    att = swa_sink_attention(q.reshape(bsz, lp, ATT_HEADS, ATT_HEADDIM),
                             k.reshape(bsz, lp, ATT_KV_HEADS, ATT_HEADDIM),
                             v.reshape(bsz, lp, ATT_KV_HEADS, ATT_HEADDIM), rel_bias, sinks)
    y_att = att @ w_attn_branch.astype(h.dtype)
    gb = gate_b.astype(h.dtype)
    merged = jax.nn.sigmoid(g_ssd + gb[0]) * y_ssd + jax.nn.sigmoid(g_att + gb[1]) * y_att
    return merged @ w_out.astype(h.dtype)

def conv_ffn(h, norm_w, w_in, conv_w, conv_b, w_down):
    u = rmsnorm(h, norm_w)
    hid = causal_dwconv(u @ w_in.astype(u.dtype), conv_w, conv_b)
    up, gate = jnp.split(hid, 2, axis=-1)
    return (jax.nn.silu(gate) * up) @ w_down.astype(h.dtype)

def second_inputs(seed: int = 0) -> dict:
    key = jax.random.key(seed)
    ks = jax.random.split(key, 24)
    f32 = jnp.float32
    nrm = lambda k, shape, s: jax.random.normal(k, shape, f32) * s
    dt0 = jnp.exp(jax.random.uniform(ks[5], (DEPTH_2, SSD_HEADS), f32, math.log(1e-3), math.log(1e-1)))
    return {
        'x': nrm(ks[0], (BATCH, SEQ, D_MODEL), 1.0),
        'meta_tokens': nrm(ks[1], (N_META, D_MODEL), 1.0),
        'norm_mix_w': 1.0 + nrm(ks[2], (DEPTH_2, D_MODEL), 0.05),
        'w_in': nrm(ks[3], (DEPTH_2, D_MODEL, D_IN_PROJ), D_MODEL ** -0.5),
        'ssd_conv_w': nrm(ks[4], (DEPTH_2, SSD_CONV, SSD_XBC), SSD_CONV ** -0.5),
        'ssd_conv_b': nrm(ks[6], (DEPTH_2, SSD_XBC), 0.01),
        'ssd_dt_bias': dt0 + jnp.log(-jnp.expm1(-dt0)),
        'ssd_a_log': jnp.log(jax.random.uniform(ks[7], (DEPTH_2, SSD_HEADS), f32, 1.0, 16.0)),
        'ssd_d': 1.0 + nrm(ks[8], (DEPTH_2, SSD_HEADS), 0.1),
        'ssd_norm_w': 1.0 + nrm(ks[9], (DEPTH_2, SSD_INNER), 0.05),
        'w_ssd_branch': nrm(ks[10], (DEPTH_2, SSD_INNER, D_MODEL), SSD_INNER ** -0.5),
        'w_attn_branch': nrm(ks[11], (DEPTH_2, ATT_Q, D_MODEL), ATT_Q ** -0.5),
        'attn_sinks': nrm(ks[12], (DEPTH_2, ATT_HEADS), 0.5),
        'rel_bias': nrm(ks[13], (REL_BUCKETS, ATT_HEADS), 0.5),
        'gate_b': nrm(ks[14], (DEPTH_2, N_BRANCH, D_MODEL), 0.1),
        'w_out': nrm(ks[15], (DEPTH_2, D_MODEL, D_MODEL), D_MODEL ** -0.5),
        'norm_ffn_w': 1.0 + nrm(ks[16], (DEPTH_2, D_MODEL), 0.05),
        'w_ffn_in': nrm(ks[17], (DEPTH_2, D_MODEL, 2 * D_FF_2), D_MODEL ** -0.5),
        'ffn_conv_w': nrm(ks[18], (DEPTH_2, FFN_CONV, 2 * D_FF_2), FFN_CONV ** -0.5),
        'ffn_conv_b': nrm(ks[19], (DEPTH_2, 2 * D_FF_2), 0.01),
        'w_ffn_out': nrm(ks[20], (DEPTH_2, D_FF_2, D_MODEL), D_FF_2 ** -0.5),
        'norm_final_w': 1.0 + nrm(ks[21], (D_MODEL,), 0.05),
    }

def second_block(x, meta_tokens, norm_mix_w, w_in, ssd_conv_w, ssd_conv_b, ssd_dt_bias, ssd_a_log, ssd_d,
              ssd_norm_w, w_ssd_branch, w_attn_branch, attn_sinks, rel_bias, gate_b, w_out, norm_ffn_w,
              w_ffn_in, ffn_conv_w, ffn_conv_b, w_ffn_out, norm_final_w):
    bsz, seq = x.shape[:2]
    lp = seq + BLOCK
    meta = jnp.broadcast_to(meta_tokens.astype(x.dtype)[None], (bsz, N_META, D_MODEL))
    h = jnp.concatenate([jnp.zeros((bsz, PAD, D_MODEL), x.dtype), meta, x], axis=1)
    valid = jnp.arange(lp) >= PAD
    valid_f32 = valid.astype(jnp.float32)
    valid_h = valid.astype(x.dtype)[None, :, None]
    for i in range(DEPTH_2):
        h = h + valid_h * mixer_block(h, valid_f32, norm_mix_w[i], w_in[i], ssd_conv_w[i], ssd_conv_b[i],
                                      ssd_dt_bias[i], ssd_a_log[i], ssd_d[i], ssd_norm_w[i], w_ssd_branch[i],
                                      w_attn_branch[i], attn_sinks[i], rel_bias, gate_b[i], w_out[i])
        h = h + valid_h * conv_ffn(h, norm_ffn_w[i], w_ffn_in[i], ffn_conv_w[i], ffn_conv_b[i], w_ffn_out[i])
    y = rmsnorm(h, norm_final_w)
    return y[:, BLOCK:]


def setup_inputs(seed=0):
    out = dict(first_inputs(seed))
    for name, value in second_inputs(seed + 1).items():
        if name != "x":
            out[name + "_2"] = value
    return out


def reference(
    x, rel_bias, norm_mix, norm_mlp, mlp_w1, mlp_w2, a_w_in, a_conv_w, a_w_out, kv_norm, w_kv,
    cmp_pe_k, cmp_pe_v, phi_k_w1, phi_k_w2, phi_v_w1, phi_v_w2, b_w_qg, b_w_o, final_norm,
    meta_tokens_2, norm_mix_w_2, w_in_2, ssd_conv_w_2, ssd_conv_b_2, ssd_dt_bias_2, ssd_a_log_2,
    ssd_d_2, ssd_norm_w_2, w_ssd_branch_2, w_attn_branch_2, attn_sinks_2, rel_bias_2, gate_b_2,
    w_out_2, norm_ffn_w_2, w_ffn_in_2, ffn_conv_w_2, ffn_conv_b_2, w_ffn_out_2, norm_final_w_2,
):
    x = first_block(
        x, rel_bias, norm_mix, norm_mlp, mlp_w1, mlp_w2, a_w_in, a_conv_w, a_w_out, kv_norm,
        w_kv, cmp_pe_k, cmp_pe_v, phi_k_w1, phi_k_w2, phi_v_w1, phi_v_w2, b_w_qg, b_w_o,
        final_norm,
    )
    return second_block(
        x, meta_tokens_2, norm_mix_w_2, w_in_2, ssd_conv_w_2, ssd_conv_b_2, ssd_dt_bias_2,
        ssd_a_log_2, ssd_d_2, ssd_norm_w_2, w_ssd_branch_2, w_attn_branch_2, attn_sinks_2,
        rel_bias_2, gate_b_2, w_out_2, norm_ffn_w_2, w_ffn_in_2, ffn_conv_w_2, ffn_conv_b_2,
        w_ffn_out_2, norm_final_w_2,
    )


_drawn_inputs = setup_inputs


def setup_inputs(seed=0):
    import zlib

    import numpy as np

    out = dict(_drawn_inputs(seed))
    spreads = {}
    factors = {'cmp_pe_k': 23.746,
     'ssd_conv_b_2': 8.0,
     'attn_sinks_2': 8.0,
     'ffn_conv_b_2': 8.0,
     'gate_b_2': 2.68}
    for name, (base, spread) in spreads.items():
        noise = np.random.default_rng([zlib.crc32(name.encode()), seed]).standard_normal(out[name].shape)
        drawn = base * np.exp(spread * noise) if base else spread * noise
        out[name] = __import__('jax').numpy.asarray(drawn.astype(out[name].dtype))
    for name, factor in factors.items():
        out[name] = (out[name] * factor).astype(out[name].dtype)
    return out
```

```python
import math
from contextlib import ExitStack, contextmanager

import numpy as np

import concourse.bass as bass
from concourse import mybir

F32 = mybir.dt.float32
F32R = mybir.dt.float32r
ALU = mybir.AluOpType
ACT = mybir.ActivationFunctionType
AX = mybir.AxisListType

P = 128
D = 1024
KT = D // P
SEQ = 512
N_META = 16
TOK = N_META + SEQ
HALF = TOK // 2
EPS = 1e-6
MASKED = -1e30

DFF = 4 * D
HEADS = 16
DH = 64
GROUPS = 4
HPG = HEADS // GROUPS
N_CMP = 31
CMP_PAD = 32
CMP_STRIDE = 16
CMP_BLOCK = 32
PHI = 256
BUCKETS = 32
REL = BUCKETS + 1
CMP_LEN = CMP_PAD + SEQ // CMP_STRIDE - 1
BAND_LEN = SEQ + P - 1
TAB1 = BAND_LEN + CMP_STRIDE * CMP_LEN
MAX_DIST = 128
QT = SEQ // P
SPAN = P * QT * (QT + 1) // 2

SSD_INNER = 2 * D
SSD_HEADS = 32
SSD_GROUPS = 4
SSD_HPG = SSD_HEADS // SSD_GROUPS
STATE = 128
SSD_TAPS = 4
DFF2 = 2816
FFT = DFF2 // P
FF_CUT = 12
KV2 = 2
WINDOW2 = 128
CHUNKS = [(0, N_META)] + [(N_META + c * P, P) for c in range(QT)]
NC = len(CHUNKS)
SCAN_AT = {7 + 6 * gg + c: (gg, c) for gg in range(2) for c in range(NC)}
ROW = 1 + N_META + 2 * P
ROW1 = 1 + N_META + P
ROW0 = 1 + N_META
BAND2 = ROW0
META2 = BAND2 + 3 * P - 1
OWN2 = META2 + P + N_META - 1
TAB2 = OWN2 + 2 * N_META - 1
TAB = TAB1 + TAB2
TAB_CUTS = [(a, min(a + 512, TAB1)) for a in range(0, TAB1, 512)] + [(a, min(a + 512, TAB)) for a in range(TAB1, TAB, 512)]
REL2 = REL + 1
DT, CS, DECAY, CDEC = range(4)
HV = 2 * 6 * 5 + 2 * KT

LAYERS = [
    ("conv_in", 12, 2), ("conv_out", 4, 2), ("mlp0", 32, 2), ("kv", 6, 2), ("phi", 4, 1),
    ("gate", 1, 1), ("qo", 8, 5), ("mlp1", 32, 2),
    ("dt", 1, 1), ("half", 28, 2), ("kv2", 1, 2), ("pair", 12, 2), ("att", 4, 2), ("out", 4, 2),
    ("ff_in0", FF_CUT, 2), ("ff_out0", KT, 1), ("ff_in1", FFT - FF_CUT, 2), ("ff_out1", KT, 1),
]
U0, T0 = {}, {}
_u, _t = 0, len(TAB_CUTS)
for _name, _n, _m in LAYERS:
    U0[_name], T0[_name] = _u, _t
    _u += _n
    _t += _n * _m
NU, NT = _u, _t
TILES = 16
MLP_TILES = DFF // P
UCOLS = TILES * P

VEC = {}
_c = 0
for _name, _n in [
    ("norm_mix0", KT), ("norm_mix1", KT), ("norm_mlp0", KT), ("norm_mlp1", KT), ("kv_norm", KT),
    ("final0", KT), ("conv_w", 3 * KT), ("pe_k", 16), ("pe_v", 16),
    ("norm_mix2", KT), ("norm_ffn", KT), ("final2", KT), ("half", 2 * HV), ("gate_b", 2 * KT), ("fconv", 8 * FFT),
    ("dt_bias", 1), ("a_log", 1), ("eps", 1), ("has_any", 1), ("quarter", QT),
]:
    VEC[_name] = _c
    _c += _n
NVEC = _c


class Link:

    def __init__(self, eng, sem):
        self.eng, self.sem, self.n, self.i, self.per, self.start = eng, sem, 0, None, 0, 0

    def at(self):
        if self.i is None:
            return self.n
        return self.i * self.per + self.n

    def mark(self, ins):
        ins.then_inc(self.sem, 1)
        self.n += 1
        return self.at()

    def wait(self, value=None):
        self.eng.wait_ge(self.sem, self.at() if value is None else value)

    @contextmanager
    def loop(self, iters, per):
        self.start = self.n
        with self.eng.Fori(0, iters) as i:
            self.i, self.per = i, per
            yield i
        assert self.n - self.start == per, (self.n - self.start, per)
        self.i = None
        self.n = self.start + per * iters


def program(nc, io):
    ctx = ExitStack()
    with ctx:
        def sb(name, shape, dt=F32, where=ctx):
            return where.enter_context(nc.sbuf_tensor(name, shape, dt))

        def sem(name):
            return ctx.enter_context(nc.semaphore(name))

        X = sb("X", [P, KT, TOK])
        parts = sb("parts", [P, 2, KT, TOK], F32R)
        Hhi, Hlo = parts[:, 0, :, :], parts[:, 1, :, :]
        R = sb("R", [P, TOK])
        R2 = sb("R2", [P, TOK])
        acc = sb("acc", [P, TOK])
        sq = sb("sq", [P, 2, TOK])
        raw = sb("raw", [P, 2, UCOLS])
        whi = sb("whi", [P, 2, UCOLS], F32R)
        wlo = sb("wlo", [P, 2, UCOLS], F32R)
        vecs = sb("vecs", [P, NVEC])
        consts = sb("consts", [P, 3, P])
        ident, ones, causal = consts[:, 0, :], consts[:, 1, :], consts[:, 2, :]
        ps = ctx.enter_context(nc.psum_tensor("ps", [P, 8, 512], F32))

        with ExitStack() as scope:
            ct = sb("ct", [P, 2, SEQ], F32, scope)
            vbuf = sb("vbuf", [P, 2, SEQ + 2], F32, scope)
            cv = sb("cv", [P, 2, SEQ], F32, scope)
            gt = sb("gt", [P, 2, SEQ], F32, scope)
            Ghi = sb("Ghi", [P, KT, SEQ], F32R, scope)
            Glo = sb("Glo", [P, KT, SEQ], F32R, scope)
            rel = sb("rel", [REL, HEADS], F32, scope)
            rel2 = sb("rel2", [REL2, HEADS], F32, scope)
            buckets = sb("buckets", [REL2, TAB], F32, scope)
            table = sb("table", [HEADS, TAB], F32, scope)
        with ExitStack() as scope:
            mt = sb("mt", [P, 2, SEQ], F32, scope)
            mid = sb("mid", [P, 2, SEQ], F32, scope)
            Mhi = sb("Mhi", [P, KT, SEQ], F32R, scope)
            Mlo = sb("Mlo", [P, KT, SEQ], F32R, scope)

        with ExitStack() as scope:
            Kd = sb("Kd", [P, 2, GROUPS, SEQ], F32, scope)
            Vt = sb("Vt", [P, 2, QT, GROUPS * DH], F32, scope)
            hid = sb("hid", [P, 2, 2, GROUPS, CMP_PAD], F32, scope)
            hidv = sb("hidv", [P, 2, GROUPS, QT, CMP_PAD], F32, scope)
            kcmp = sb("kcmp", [P, GROUPS, CMP_PAD], F32, scope)
            vcmp = sb("vcmp", [P, GROUPS, DH], F32, scope)
            w2 = sb("w2", [P, 2, P + DH], F32, scope)
            gates = sb("gates", [P, QT, 3 * HEADS], F32, scope)
            ctab = sb("ctab", [P, HEADS, QT * CMP_PAD], F32, scope)
            with ExitStack() as part:
                Vf = sb("Vf", [P, 2, SEQ], F32, part)
                kcat = sb("kcat", [P, 2, GROUPS, SEQ + 1], F32, part)
                phi_hi = sb("phi_hi", [P, 2, 16, GROUPS * N_CMP], F32R, part)
                phi_lo = sb("phi_lo", [P, 2, 16, GROUPS * N_CMP], F32R, part)
                gf = sb("gf", [P, SEQ], F32, part)
            near = sb("near", [P, HPG, SEQ], F32, scope)
            Qs = sb("Qs", [P, 2, SEQ], F32, scope)
            Ks = sb("Ks", [P, 2, SEQ], F32, scope)
            Vs = sb("Vs", [P, 2, QT, DH], F32, scope)
            kcs = sb("kcs", [P, CMP_PAD], F32, scope)
            vcs = sb("vcs", [P, QT, DH], F32, scope)
            Ohi = sb("Ohi", [P, 2, SEQ], F32R, scope)
            Olo = sb("Olo", [P, 2, SEQ], F32R, scope)
            Sb = sb("Sb", [P, 2, SPAN], F32, scope)
            PT = sb("PT", [P, SPAN], F32, scope)
            Sc = sb("Sc", [P, HPG * QT, CMP_PAD], F32, scope)
            PTc = sb("PTc", [P, HPG, P], F32, scope)
            nmax = sb("nmax", [P, 2, QT], F32, scope)
            rsum = sb("rsum", [P, 2, QT], F32, scope)
            coef = sb("coef", [P, 2, QT], F32, scope)
            cst = sb("cst", [P, 3, HPG * QT], F32, scope)
        with ExitStack() as rest:
            with ExitStack() as scope:
                YS = sb("YS", [P, KT, TOK], F32, scope)
                tok = sb("tok", [P, 4, NC, SSD_HEADS], F32, scope)
                tokh = sb("tokh", [P, 4, NC, SSD_HEADS // 2], F32, scope)
                hv = sb("hv", [P, HV], F32, scope)
                with ExitStack() as part:
                    dts = sb("dts", [SSD_HEADS, 2, TOK], F32, part)
                    dtw = sb("dtw", [SSD_HEADS, 6, TOK], F32, part)
                    al = sb("al", [SSD_HEADS, 1], F32, part)
                Y = sb("Y", [P, KT, TOK], F32, scope)
                stg = sb("stg", [P, 2, SSD_TAPS - 1 + TOK], F32, scope)
                Gv = sb("Gv", [P, 2, TOK], F32, scope)
                Gr = sb("Gr", [P, TOK], F32, scope)
                with ExitStack() as part:
                    YNhi = sb("YNhi", [P, KT, TOK], F32R, part)
                    YNlo = sb("YNlo", [P, KT, TOK], F32R, part)
                BC = sb("BC", [P, 2, 2, TOK], F32, scope)
                csb = sb("csb", [P, 2, SSD_HPG, P], F32, scope)
                csf = sb("csf", [P, 2, SSD_HPG // 2, P], F32, scope)
                L = sb("L", [P, 2, SSD_HPG, P], F32, scope)
                ecs = sb("ecs", [P, 2, SSD_HPG // 2, P], F32, scope)
                xdt = sb("xdt", [P, SSD_HPG * DH], F32, scope)
                xdd = sb("xdd", [P, SSD_HPG * DH], F32, scope)
                yoff = sb("yoff", [P, SSD_HPG // 2, P], F32, scope)
                Btok = sb("Btok", [P, P], F32, scope)
                cbm = sb("cbm", [P, P], F32, scope)
                Hs = sb("Hs", [P, SSD_HPG * DH], F32, scope)
                Hd = sb("Hd", [P, SSD_HPG * DH], F32, scope)
            with ExitStack() as scope:
                sb("over_YS", [P, KT, TOK], F32, scope)
                GA = sb("GA", [P, KT, TOK], F32, scope)
                AThi = sb("AThi", [P, KT, TOK], F32R, scope)
                ATlo = sb("ATlo", [P, KT, TOK], F32R, scope)
                Q2 = sb("Q2", [P, 2, TOK], F32, scope)
                Kd2 = sb("Kd2", [P, KV2, 1 + TOK], F32, scope)
                Vt2 = sb("Vt2", [P, NC, KV2 * DH], F32, scope)
                Ks2 = sb("Ks2", [P, 1 + TOK], F32, scope)
                Vs2 = sb("Vs2", [P, NC, DH], F32, scope)
                tabs = sb("tabs", [P, 2, ROW + ROW1], F32, scope)
                tab0 = sb("tab0", [N_META, 2, ROW0], F32, scope)
                Pb = sb("Pb", [P, 2, ROW], F32, scope)
                Pb0 = sb("Pb0", [P, 2, ROW0], F32, scope)
                PT2 = sb("PT2", [P, 2 * P], F32, scope)
                PTm = sb("PTm", [N_META, P], F32, scope)
                PT0 = sb("PT0", [N_META, 2 * N_META], F32, scope)
                nmax2 = sb("nmax2", [P, 4], F32, scope)
                rsum2 = sb("rsum2", [P, 4], F32, scope)
            with ExitStack() as scope:
                Fhi = sb("Fhi", [P, FF_CUT, TOK], F32R, scope)
                sb("over_GA", [P, 2 * KT - FF_CUT, TOK], F32, scope)
                sb("over_AT", [P, 2 * KT, TOK], F32, scope)
                Fstg = sb("Fstg", [P, 2, 2 + TOK], F32, scope)
                Fcv = sb("Fcv", [P, 2, TOK], F32, scope)
        Flo = parts.rearrange("p a k n -> p (a k) n")
        scratch = nc.dram_tensor("scratch", [HEADS, TAB], F32).ap()
        bands = nc.dram_tensor("bands", [HEADS, P, SEQ], F32).ap()
        bands2 = nc.dram_tensor("bands2", [HEADS, P, ROW + ROW1], F32).ap()
        bands0 = nc.dram_tensor("bands0", [HEADS, N_META, ROW0], F32).ap()
        sums_d = nc.dram_tensor("sums_d", [SSD_HEADS, TOK], F32).ap()

        x_loaded, vecs_loaded = sem("x_loaded"), sem("vecs_loaded")
        landed = [sem("landed0"), sem("landed1")]
        hi_done, lo_done = sem("hi_done"), sem("lo_done")
        mt_full, mt_free = sem("mt_full"), sem("mt_free")
        x_new = sem("x_new")
        h_hi, h_ready = sem("h_hi"), sem("h_ready")
        sq_done, sq_add = sem("sq_done"), sem("sq_add")
        ssum, variance, rms, rstd = sem("ssum"), sem("variance"), sem("rms"), sem("rstd")
        g_hi, g_ready = sem("g_hi"), sem("g_ready")
        m_new, m_hi, m_ready = sem("m_new"), sem("m_hi"), sem("m_ready")
        dve_own, act_own = sem("dve_own"), sem("act_own")
        stored = sem("stored")
        tab_loaded, tab_stored = sem("tab_loaded"), sem("tab_stored")
        phi_h, phi_ready = sem("phi_h"), sem("phi_ready")
        dup = [sem(f"dup{n}") for n in range(4)]
        vt_full, vt_free = sem("vt_full"), sem("vt_free")
        ctab_loaded, hid_ready = sem("ctab_loaded"), sem("hid_ready")
        cmp_full, cmp_ready = sem("cmp_full"), sem("cmp_ready")
        gate_sig, gate_full, gate_ready = sem("gate_sig"), sem("gate_full"), sem("gate_ready")
        sink_stored, band_stored, near_loaded, staged = sem("sink_stored"), sem("band_stored"), sem("near_loaded"), sem("staged")
        cs_full, c_new, c_exp, pc_ready = sem("cs_full"), sem("c_new"), sem("c_exp"), sem("pc_ready")
        ctr_full, ptc_ready = sem("ctr_full"), sem("ptc_ready")
        ttr_done, exp_done = sem("ttr_done"), sem("exp_done")
        coef_ready, p_ready = sem("coef_ready"), sem("p_ready")
        pt_full, pt_act, pt_dve = sem("pt_full"), sem("pt_act"), sem("pt_dve")
        o_full, o_hi, o_ready = sem("o_full"), sem("o_hi"), sem("o_ready")

        cs_new, cs_stored, dt_abs, dt_exp = sem("cs_new"), sem("cs_stored"), sem("dt_abs"), sem("dt_exp")
        tok_full, tok_new, cl_full, tok_diff, tok_ready = sem("tok_full"), sem("tok_new"), sem("cl_full"), sem("tok_diff"), sem("tok_ready")
        tokh_ready, xbc_new, xs_ready = sem("tokh_ready"), sem("xbc_new"), sem("xs_ready")
        cs_loaded = [sem("cs_loaded0"), sem("cs_loaded1")]
        cb_ready = sem("cb_ready")
        l_ready, ecs_ready, a_full, btok_ready = sem("l_ready"), sem("ecs_ready"), sem("a_full"), sem("btok_ready")
        decayed, xd_ready, y_full, y_done = sem("decayed"), sem("xd_ready"), sem("y_full"), sem("y_done")
        st_full, h_new, hd_ready = sem("st_full"), sem("h_new"), sem("hd_ready")
        z_silu, z_new, z_sq, z_add = sem("z_silu"), sem("z_new"), sem("z_sq"), sem("z_add")
        gsum, gvar, gsqrt = sem("gsum"), sem("gvar"), sem("gsqrt")
        yn_new, yn_hi, yn_ready = sem("yn_new"), sem("yn_hi"), sem("yn_ready")
        kdup, v_full, kv_staged, tabs_loaded = sem("kdup"), sem("v_full"), sem("kv_staged"), sem("tabs_loaded")
        ga_new = sem("ga_new")
        gs_new, gs_sig, ttr2, exp2, p2_ready = sem("gs_new"), sem("gs_sig"), sem("ttr2"), sem("exp2"), sem("p2_ready")
        pt2_full, pt2_dve, o2_full, at_ready = sem("pt2_full"), sem("pt2_dve"), sem("o2_full"), sem("at_ready")
        ga_sig, mg_new, mg_hi, mg_ready = sem("ga_sig"), sem("mg_new"), sem("mg_hi"), sem("mg_ready")
        f_new, f_silu, f_hi, f_ready = sem("f_new"), sem("f_silu"), sem("f_hi"), sem("f_ready")
        out_new = sem("out_new")

        block = ctx.enter_context(nc.Block())

        def vec(name, k=0, n=1):
            return vecs[:, VEC[name] + k:VEC[name] + k + n]

        def vec_at(name, k):
            return vecs[:, VEC[name] + k:VEC[name] + k + 1] if isinstance(k, int) else vecs[:, bass.ds(k + VEC[name], 1)]

        def t_at(buf, k, a=0, b=None):
            b = buf.shape[2] if b is None else b
            if isinstance(k, int):
                return buf[:, k, a:b]
            return buf[:, bass.ds(k, 1), a:b].rearrange("p a n -> p (a n)")

        def first(t):
            return P * t * (t + 1) // 2

        def turn_at(t, k):
            bank, at = ((3, 0), (4, 0), (5, 0), (4, 3 * P))[k]
            return bank, at + (t - k) * P

        KEYS_AT = (0, SEQ, 2 * SEQ, SEQ + 3 * P)

        def block_rows(kv, k):
            return kcat[:, kv, :, 1 + 2 * k:1 + 2 * k + CMP_STRIDE * (N_CMP - 1) + 1:CMP_STRIDE]

        def halves(ap):
            return ap.rearrange("p (h n) -> p h n", h=2)

        def halves_at(buf, k):
            return buf[:, bass.ds(k, 1), :].rearrange("p a (h n) -> p (a h) n", h=2)

        def product(par, rows=slice(0, P)):
            return ps[rows, 2 * par:2 * par + 2, 0:HALF]

        def conv_out(r):
            gg, t = r // 6, r % 6
            return BC[:, gg, t, :] if t < 2 else Y[:, 4 * gg + t - 2, :]

        def conv_vec(r, tap):
            return hv[:, r * 5 + tap:r * 5 + tap + 1]

        def skip_vec(q):
            return hv[:, 60 + q:61 + q]

        def gain_vec(q):
            return hv[:, 60 + KT + q:61 + KT + q]

        SUMS = 6
        SUMS2 = ps[:, SUMS:SUMS + 2, 0:HALF]
        R1 = R[:, N_META:TOK]
        @block.sync
        def _(sp):
            sp.dma_start(X[:, :, N_META:TOK], io["x"]).then_inc(x_loaded, 16)
            sp.dma_start(X[:, :, 0:N_META], io["meta"]).then_inc(x_loaded, 16)
            for s in range(2):
                sp.dma_start(raw[:, s, :], io["stream"][s]).then_inc(landed[s], 16)
            with sp.Fori(1, NU // 2) as i:
                for s in range(2):
                    sp.wait_ge(lo_done, i * 2 + (s - 1))
                    src = io["stream"][bass.ds(i * 2 + s, 1), :, :].rearrange("a p n -> p (a n)")
                    sp.dma_start(raw[:, s, :], src).then_inc(landed[s], 16)
            if NU % 2:
                sp.wait_ge(lo_done, NU - 2)
                sp.dma_start(raw[:, 0, :], io["stream"][NU - 1]).then_inc(landed[0], 16)

        @block.gpsimd
        def _(pool):
            def split_low(u, s):
                pool.wait_ge(hi_done, u + 1)
                nc.gpsimd.tensor_tensor(wlo[:, s, :], raw[:, s, :], whi[:, s, :].bitcast(F32),
                                        ALU.subtract).then_inc(lo_done, 1)

            def split_units(a, b):
                if a % 2 and a < b:
                    split_low(a, 1)
                    a += 1
                if b - a > 1:
                    with pool.Fori(0, (b - a) // 2) as i:
                        for s in range(2):
                            split_low(i * 2 + (a + s), s)
                if (b - a) % 2:
                    split_low(b - 1, 0)

            split_units(0, U0["qo"] + 1)
            with pool.Fori(0, GROUPS) as g:
                split_low(g * 2 + (U0["qo"] + 1), (U0["qo"] + 1) % 2)
                for n in (2, 3):
                    pool.wait_ge(dup[n], 64)
                pool.wait_ge(vt_free, 4)
                pool.wait_ge(cmp_ready, 2)
                for br in range(2):
                    nc.gpsimd.tensor_copy(Ks[:, br, :], t_at(Kd[:, br, :, :], g))
                    nc.gpsimd.tensor_copy(Vs[:, br, :, :], Vt[:, br, :, bass.ds(g * DH, DH)])
                nc.gpsimd.tensor_copy(kcs[:, :], t_at(kcmp, g))
                for t in range(QT):
                    copy = nc.gpsimd.tensor_tensor(vcs[:, t, :], t_at(vcmp, g), vec("quarter", t).to_broadcast([P, DH]), ALU.mult)
                copy.then_inc(staged, 1)
                split_low(g * 2 + (U0["qo"] + 2), U0["qo"] % 2)
                for r in range(8):
                    pool.wait_ge(coef_ready, g * 8 + (r + 1))
                    for t in range(QT):
                        row = Sb[:, r % 2, first(t):first(t + 1)]
                        scale = coef[:, r % 2, t:t + 1].to_broadcast([P, (t + 1) * P])
                        nc.gpsimd.tensor_tensor(row, row, scale, ALU.mult).then_inc(p_ready, 1)
            split_units(U0["qo"] + 9, U0["half"] + 2)
            pool.wait_ge(tok_ready, 1)
            with pool.Fori(0, 2) as i:
                for r in range(1, 29):
                    if r % 2 == 0:
                        u = U0["half"] + r // 2 + 1
                        split_low(i * 14 + u, u % 2)
                    gg, c = SCAN_AT.get(r, (0, NC))
                    if c < NC - 2:
                        pool.wait_ge(h_new, i * 8 + (4 * gg + c + 1))
                        if gg + c == 0:
                            pool.wait_ge(tokh_ready, i + 1)
                        heads = [P, SSD_HPG, DH]
                        decay = tokh[:, CDEC, c + 1, gg * SSD_HPG:(gg + 1) * SSD_HPG].unsqueeze(2).to_broadcast(heads)
                        nc.gpsimd.tensor_tensor(Hd[:, :].rearrange("p (h d) -> p h d", h=SSD_HPG), Hs[:, :].rearrange("p (h d) -> p h d", h=SSD_HPG),
                                                decay, ALU.mult).then_inc(hd_ready, 1)
            split_units(U0["half"] + 30, NU)

        @block.scalar
        def _(act):
            act.dma_start(vecs[:, :], io["vecs"]).then_inc(vecs_loaded, 16)
            act.dma_start(consts[:, :, :], io["consts"]).then_inc(vecs_loaded, 16)
            act.dma_start(rel[:, :], io["rel"]).then_inc(tab_loaded, 16)
            act.dma_start(rel2[:, :], io["rel2"]).then_inc(tab_loaded, 16)
            act.dma_start(buckets[:, :], io["buckets"]).then_inc(tab_loaded, 16)

            def split_high(s, half):
                act.wait_ge(landed[s], half * 16 + 16)
                nc.scalar.activation(whi[:, s, :], raw[:, s, :], ACT.Copy).then_inc(hi_done, 1)

            def next_unit(layer, c, m=2, turn=0, half_turn=0):
                act.wait_ge(mt_full, turn * m + (T0[layer] + m * (c + 1)))
                u = U0[layer] + c + 2
                split_high(u % 2, half_turn + u // 2)

            def norm_tile(n, part, k, slot, gain, after, a=N_META, hi=Hhi):
                act.wait_ge(*after)
                if gain:
                    nc.scalar.activation(hi[:, k, a:], X[:, k, a:], ACT.Identity, scale=vec(gain, k)).then_inc(h_hi, 1)
                if n or k >= 2:
                    act.wait_ge(sq_add, k + (KT * n - 1))
                nc.scalar.activation(sq[:, slot, a:], X[:, k, a:], ACT.Square).then_inc(sq_done, 1)

            def norm_root(n, a=N_META):
                act.wait_ge(variance, n + 1)
                nc.scalar.activation(R2[:, a:], acc[:, a:], ACT.Sqrt).then_inc(rms, 1)

            def mlp(layer, n, part, gain):
                base = 0 if layer == "mlp0" else MLP_TILES
                def quarter(c, last):
                    for j in range(4):
                        next_unit(layer, j, turn=c * 8, half_turn=c * 4)
                        for m in range(2):
                            act.wait_ge(m_new, c * KT + (base + 2 * j + m + 1))
                            nc.scalar.activation(Mhi[:, 2 * j + m, :], mid[:, m, :], ACT.Copy).then_inc(m_hi, 1)
                    for j in range(4):
                        next_unit(layer, 4 + j, turn=c * 8, half_turn=c * 4)
                        for m in range(2 if last else 0):
                            t = 2 * j + m
                            norm_tile(n, part, t, m, gain, (mt_free, T0[layer] + 64 - 8 + t + 1))
                with act.Fori(0, 3) as c:
                    quarter(c, False)
                quarter(3, True)
                norm_root(n)

            act.wait_ge(vecs_loaded, 32)
            for k in range(KT):
                norm_tile(0, 0, k, k % 2, "norm_mix0", (x_loaded, 32))
            for s in range(2):
                split_high(s, 0)
            norm_root(0)
            act.wait_ge(mt_free, len(TAB_CUTS))
            act.dma_start(scratch, table[:, :]).then_inc(tab_stored, 16)
            with act.Fori(0, 2) as i:
                for c in range(6):
                    next_unit("conv_in", c, turn=i * 6, half_turn=i * 3)
            for c in range(4):
                next_unit("conv_out", c)
                for m in range(2):
                    norm_tile(1, 1, 2 * c + m, m, "norm_mlp0", (mt_free, T0["conv_out"] + 2 * c + m + 1))
            norm_root(1)
            mlp("mlp0", 2, 2, "kv_norm")
            act.dma_start(w2[:, :, :], io["phi_w2"]).then_inc(ctab_loaded, 16)
            act.wait_ge(tab_stored, 16)
            def spread(to, at, rows, cols, step=-1, done=band_stored):
                act.dma_start(to, bass.AP(scratch.tensor, at, [[TAB, HEADS], [step, rows], [1, cols]])).then_inc(done, 16)

            two = TAB1
            spread(bands2[:, :, 0:ROW0], two, P, ROW0, 0, sink_stored)
            spread(bands2[:, :, ROW:ROW + ROW0], two, P, ROW0, 0, sink_stored)
            spread(bands0[:, :, :], two, N_META, ROW0, 0, sink_stored)
            spread(bands2[:, :, ROW0:ROW], two + BAND2 + P - 1, P, 2 * P)
            spread(bands2[:, :, ROW + ROW0:], two + BAND2 + 2 * P - 1, P, P)
            spread(bands[:, :, :], P - 1, P, SEQ)
            for a in range(P // CMP_STRIDE):
                for t in range(QT):
                    act.dma_start(
                        ctab[CMP_STRIDE * a:CMP_STRIDE * (a + 1), :, t * CMP_PAD:(t + 1) * CMP_PAD],
                        bass.AP(scratch.tensor, BAND_LEN + SEQ // CMP_STRIDE - 1 - a - P // CMP_STRIDE * t,
                                [[CMP_LEN, CMP_STRIDE], [TAB, HEADS], [1, CMP_PAD]]),
                    ).then_inc(ctab_loaded, 16)

            act.wait_ge(sink_stored, 48)
            spread(bands2[:, :, ROW + 1:ROW + ROW0], two + META2 + P - 1, P, N_META)
            spread(bands0[:, :, 1:], two + OWN2 + N_META - 1, N_META, N_META)

            def copy_halves(c):
                n = (0, 1, 2, None, 3)[c]
                for m in range(2):
                    act.wait_ge(mt_free, T0["kv"] + 2 * c + m + 1)
                    if c < 2:
                        lows, highs = kcat[0:DH, c, :, 1:SEQ + 1], kcat[DH:P, c, :, 0:SEQ]
                        act.dma_start(highs[:, 2 * m, :], lows[:, 2 * m, :]).then_inc(dup[n], 16)
                        act.dma_start(lows[:, 2 * m + 1, :], highs[:, 2 * m + 1, :]).then_inc(dup[n], 16)
                    else:
                        br = n - 2
                        act.dma_start(Kd[DH:P, br, 2 * m, :], Kd[0:DH, br, 2 * m, :]).then_inc(dup[n], 16)
                        act.dma_start(Kd[0:DH, br, 2 * m + 1, :], Kd[DH:P, br, 2 * m + 1, :]).then_inc(dup[n], 16)

            def phi_parts(kv):
                act.wait_ge(dup[kv], 64)
                for k in range(16):
                    nc.scalar.activation(phi_hi[:, kv, k, :].rearrange("p (g n) -> p g n", g=GROUPS), block_rows(kv, k),
                                         ACT.Identity, bias=vec(("pe_k", "pe_v")[kv], k)).then_inc(phi_h, 1)

            for c in range(6):
                next_unit("kv", c)
                if c in (0, 1, 2, 4):
                    copy_halves(c)
                if c in (2, 3):
                    phi_parts(c - 2)
            for k in range(KT):
                nc.scalar.activation(Hhi[:, k, N_META:TOK], X[:, k, N_META:TOK], ACT.Identity,
                                     scale=vec("norm_mix1", k)).then_inc(h_hi, 1)
            for c in range(4):
                next_unit("phi", c, m=1)
                act.wait_ge(mt_free, T0["phi"] + c + 1)
                h = hid[:, c // 2, c % 2, :, 0:N_CMP]
                if c < 2:
                    nc.scalar.activation(h, h, ACT.Silu).then_inc(hid_ready, 1)
                for t in range(QT if c >= 2 else 0):
                    nc.scalar.activation(hidv[:, c % 2, :, t, 0:N_CMP], h, ACT.Silu).then_inc(hid_ready, 1)
            next_unit("gate", 0, m=1)
            act.wait_ge(mt_free, T0["gate"] + 1)
            nc.scalar.activation(gf[0:3 * HEADS, :], gf[0:3 * HEADS, :], ACT.Sigmoid).then_inc(gate_sig, 1)

            act.wait_ge(band_stored, 16 * 5)
            with act.Fori(0, GROUPS) as g:
                act.dma_start(near[:, :, :], bands[bass.ds(g * HPG, HPG), :, :].rearrange("h p n -> p h n")).then_inc(near_loaded, 16)
                act.wait_ge(mt_full, g * 10 + (T0["qo"] + 2))
                split_high(U0["qo"] % 2, g + (U0["qo"] + 2) // 2)
                act.wait_ge(c_new, g + 1)
                nc.scalar.activation(Sc[:, :, :], Sc[:, :, :], ACT.Exp).then_inc(c_exp, 1)

                def exps(r):
                    for t in range(QT):
                        act.wait_ge(ttr_done, g * 32 + (4 * r + t + 1))
                        row = Sb[:, r % 2, first(t):first(t + 1)]
                        nc.scalar.activation(row, row, ACT.Exp, bias=nmax[:, r % 2, t:t + 1], scale=-1.0,
                                             accum_out=rsum[:, r % 2, t:t + 1]).then_inc(exp_done, 1)

                def turned(r):
                    act.wait_ge(pt_full, g * 8 + (r + 1))
                    nc.scalar.activation(PT[:, 0:SEQ], ps[:, 3, :], ACT.Copy).then_inc(pt_act, 1)

                def heads_out(j):
                    act.wait_ge(o_full, g * 2 + (j + 1))
                    nc.scalar.activation(Ohi[:, j, :], ps[:, 6 + j, :], ACT.Copy).then_inc(o_hi, 1)

                exps(0)
                exps(1)
                for r in range(8):
                    turned(r)
                    if r < 6:
                        exps(r + 2)
                    if r == 4:
                        heads_out(0)
                heads_out(1)
                act.wait_ge(mt_full, g * 10 + (T0["qo"] + 10))
                split_high((U0["qo"] + 1) % 2, g + (U0["qo"] + 3) // 2)
            for k in range(KT):
                norm_tile(3, 4, k, k % 2, "norm_mlp1", (mt_free, T0["qo"] + 40))
            norm_root(3)

            mlp("mlp1", 4, None, None)
            for k in range(KT):
                norm_tile(5, 5, k, k % 2, "norm_mix2", (x_new, k + 1), 0)
            norm_root(5, 0)

            next_unit("dt", 0, m=1)
            nc.scalar.activation(al[:, :], vecs[0:SSD_HEADS, VEC["a_log"]:VEC["a_log"] + 1], ACT.Exp).then_inc(dt_exp, 1)
            act.wait_ge(dt_abs, 1)
            nc.scalar.activation(dtw[:, 1, :], dtw[:, 1, :], ACT.Exp, scale=-1.0).then_inc(dt_exp, 1)
            act.wait_ge(cs_new, 1)
            act.dma_start(sums_d, dts[:, 1, :]).then_inc(cs_stored, 16)
            act.wait_ge(tok_diff, 1)
            nc.scalar.activation(tok[:, DECAY, :, :], tok[:, DECAY, :, :], ACT.Exp)
            nc.scalar.activation(tok[:, CDEC, :, :], ps[:, 6, 0:NC * SSD_HEADS].rearrange("p (c h) -> p c h", c=NC), ACT.Exp).then_inc(tok_ready, 1)
            act.wait_ge(cs_stored, 16)

            own = Link(act, act_own)
            with own.loop(2, 10) as i:
                def load_sums(n):
                    gg, c = divmod(n, NC)
                    at, w = CHUNKS[c]
                    at += gg * (SSD_HPG * TOK)
                    act.dma_start(csb[0:w, n % 2, :, 0:w], bass.AP(sums_d.tensor, i * (2 * SSD_HPG * TOK) + at, [[0, w], [TOK, SSD_HPG], [1, w]])).then_inc(cs_loaded[n % 2], 16)
                    for b in range(2):
                        act.dma_start(csf[b * DH:(b + 1) * DH, n % 2, :, 0:w],
                                      bass.AP(sums_d.tensor, i * (2 * SSD_HPG * TOK) + (at + b * TOK), [[0, DH], [2 * TOK, SSD_HPG // 2], [1, w]])).then_inc(cs_loaded[n % 2], 16)

                def decays(n):
                    gg, c = divmod(n, NC)
                    w = CHUNKS[c][1]
                    act.wait_ge(cs_loaded[n % 2], i * 240 + 48 * (n // 2 + 1))
                    for h in range(SSD_HPG):
                        relu = nc.scalar.activation(L[0:w, n % 2, h, 0:w], csb[0:w, n % 2, h, 0:w], ACT.Relu, scale=-1.0,
                                                    bias=tokh[0:w, CS, c, gg * SSD_HPG + h:gg * SSD_HPG + h + 1])
                    own.mark(relu)
                    if c:
                        if n >= 2:
                            act.wait_ge(y_done, i * 10 + (n - 1))
                        nc.scalar.activation(ecs[:, n % 2, :, 0:w], csf[:, n % 2, :, 0:w], ACT.Exp).then_inc(ecs_ready, 1)
                    own.wait()
                    nc.scalar.activation(L[0:w, n % 2, :, 0:w], L[0:w, n % 2, :, 0:w], ACT.Exp, scale=-1.0).then_inc(l_ready, 1)
                    if n + 2 < 2 * NC:
                        if c:
                            act.wait_ge(ecs_ready, i * 8 + (4 * gg + c))
                        load_sums(n + 2)

                act.wait_ge(tokh_ready, i + 1)
                load_sums(0)
                load_sums(1)
                for r in range(29):
                    if r and r % 2 == 0:
                        next_unit("half", r // 2 - 1, turn=i * 14, half_turn=i * 7)
                    if r == 0:
                        decays(0)
                    if r in SCAN_AT:
                        gg, c = SCAN_AT[r]
                        n, w = gg * NC + c, CHUNKS[c][1]
                        act.wait_ge(cb_ready, i * 10 + (n + 1))
                        if c < NC - 1:
                            nc.scalar.activation(Btok[0:w, :], ps[0:w, 5, 0:P], ACT.Copy).then_inc(btok_ready, 1)
                        if n + 1 < 2 * NC:
                            decays(n + 1)
                    if 0 < r <= 12:
                        act.wait_ge(xbc_new, i * 12 + r)
                        nc.scalar.activation(conv_out(r - 1), conv_out(r - 1), ACT.Silu).then_inc(xs_ready, 1)
                    elif 12 < r <= 20:
                        q = r - 13
                        z = stg[:, q % 2, SSD_TAPS - 1:]
                        act.wait_ge(mt_free, i * 28 + (T0["half"] + r))
                        nc.scalar.activation(z, z, ACT.Silu).then_inc(z_silu, 1)
                        if r == 19:
                            act.wait_ge(gvar, i * 2 + 1)
                            nc.scalar.activation(R2[:, :], Gv[:, 0, :], ACT.Sqrt).then_inc(gsqrt, 1)
                        act.wait_ge(z_new, i * 8 + (q + 1))
                        if q >= 2:
                            act.wait_ge(z_add, i * 8 + (q - 1))
                        nc.scalar.activation(sq[:, q % 2, :], Y[:, q, :], ACT.Square).then_inc(z_sq, 1)
                    if r == 20:
                        act.wait_ge(gvar, i * 2 + 2)
                        nc.scalar.activation(R2[:, :], Gv[:, 1, :], ACT.Sqrt).then_inc(gsqrt, 1)
                    for q in range(*((0, 4) if r == 19 else (4, 8) if r == 20 else (0, 0))):
                        act.wait_ge(yn_new, i * 8 + (q + 1))
                        nc.scalar.activation(YNhi[:, q, :], Y[:, q, :], ACT.Copy).then_inc(yn_hi, 1)

            next_unit("kv2", 0)
            act.wait_ge(mt_free, T0["kv2"] + 1)
            act.dma_start(Kd2[DH:P, 0, :], Kd2[0:DH, 0, :]).then_inc(kdup, 16)
            act.dma_start(Kd2[0:DH, 1, :], Kd2[DH:P, 1, :]).then_inc(kdup, 16)
            with act.Fori(0, 2) as i:
                for p in range(4):
                    base = i * 40 + 10 * p

                    def exps(n):
                        for h in range(2 if n == 8 else 1):
                            act.wait_ge(ttr2, base + (n + h + 1))
                            if n < 8:
                                w, x = (ROW if n % 4 else ROW1), P
                                row = Pb[:, n % 2, 0:w]
                                k = n % 2
                            else:
                                row, x, k = Pb0[0:N_META, h, :], N_META, 2 + h
                            nc.scalar.activation(row, row, ACT.Exp, bias=nmax2[0:x, k:k + 1], scale=-1.0,
                                                 accum_out=rsum2[0:x, k:k + 1]).then_inc(exp2, 1)

                    act.dma_start(tabs[:, :, :], bands2[bass.ds(i * 8 + 2 * p, 2), :, :].rearrange("h p n -> p h n")).then_inc(tabs_loaded, 16)
                    act.dma_start(tab0[:, :, :], bands0[bass.ds(i * 8 + 2 * p, 2), :, :].rearrange("h p n -> p h n")).then_inc(tabs_loaded, 16)
                    for rr in (3 * p, 3 * p + 1):
                        if rr % 2:
                            next_unit("pair", rr // 2, turn=i * 6, half_turn=i * 3)
                    exps(0)
                    exps(1)
                    act.wait_ge(gs_new, i * 4 + (p + 1))
                    nc.scalar.activation(sq[:, 0, :], sq[:, 0, :], ACT.Sigmoid).then_inc(gs_sig, 1)
                    for n in range(8):
                        if n < 7:
                            exps(n + 2)
                    rr = 3 * p + 2
                    if rr % 2:
                        next_unit("pair", rr // 2, turn=i * 6, half_turn=i * 3)
            act.wait_ge(ga_new, 8)
            for k in range(KT):
                nc.scalar.activation(GA[:, k, :], GA[:, k, :], ACT.Sigmoid).then_inc(ga_sig, 1)
            for c in range(4):
                next_unit("att", c)
                for m in range(2):
                    k = 2 * c + m
                    act.wait_ge(mg_new, k + 1)
                    nc.scalar.activation(Hhi[:, k, :], sq[:, m, :], ACT.Copy).then_inc(mg_hi, 1)
            for c in range(4):
                next_unit("out", c)
                for m in range(2):
                    norm_tile(6, 6, 2 * c + m, m, "norm_ffn", (mt_free, T0["out"] + 2 * c + m + 1), 0, AThi)
            norm_root(6, 0)

            for f, (a, b) in enumerate(((0, FF_CUT), (FF_CUT, FFT))):
                with act.Fori(0, (b - a) // 2) as i:
                    for c in range(2):
                        act.wait_ge(f_new, i * 2 + (a + c + 1))
                        nc.scalar.activation(Fcv[:, 1, :], Fcv[:, 1, :], ACT.Silu).then_inc(f_silu, 1)
                        next_unit(f"ff_in{f}", c, turn=i * 2, half_turn=i)
                for c in range(KT):
                    if U0[f"ff_out{f}"] + c + 2 < NU:
                        next_unit(f"ff_out{f}", c, m=1)
                    if f:
                        norm_tile(7, None, c, c % 2, None, (mt_free, T0["ff_out1"] + c + 1), 0)
            norm_root(7, 0)
            for k in range(KT):
                act.wait_ge(out_new, k + 1)
                act.dma_start(io["out"][:, k, :], X[:, k, N_META:]).then_inc(stored, 16)
            act.wait_ge(stored, 16 * KT)

        @block.tensor
        def _(pe):
            def unit(layer, c, rhs, m_tiles=2, k_tiles=KT, turn=0, turn_m=2, ready=None, free=None):
                s = (U0[layer] + c) % 2
                pe.wait_ge(lo_done, turn + (U0[layer] + c + 1))
                pe.wait_ge(mt_free, turn * turn_m + (T0[layer] + turn_m * c - turn_m) if free is None else free)
                hi, lo = rhs
                for m in range(m_tiles):
                    out = ps[:, 2 * s + m, :]
                    for k in range(k_tiles):
                        if ready and not m:
                            pe.wait_ge(*ready(k))
                        at = slice((k * m_tiles + m) * P, (k * m_tiles + m + 1) * P)
                        for j, (w, x) in enumerate(((whi, hi), (whi, lo), (wlo, hi))):
                            mm = nc.tensor.matmul(out, w[:, s, at], x(k), start=k + j == 0,
                                                  stop=k == k_tiles - 1 and j == 2)
                    mm.then_inc(mt_full, 1)

            def tiles(hi, lo, a=0):
                return (lambda k: hi[:, k, a:]), (lambda k: lo[:, k, a:])

            def norm_sum(n):
                pe.wait_ge(sq_add, KT * n + KT)
                nc.tensor.matmul(ps[:, SUMS, :], ones, acc[:, N_META:TOK], start=True, stop=True).then_inc(ssum, 1)

            H1, G, M = tiles(Hhi, Hlo, N_META), tiles(Ghi, Glo), tiles(Mhi, Mlo)

            def mlp(layer, part):
                base = 0 if layer == "mlp0" else MLP_TILES
                def quarter(c, first):
                    for j in range(4):
                        unit(layer, j, H1, turn=c * 8, ready=(lambda k: (h_ready, KT * part + k + 1)) if first and not j else None)
                    for j in range(4):
                        unit(layer, 4 + j, M, turn=c * 8, ready=(lambda k: (m_ready, c * KT + (base + k + 1))) if not j else None)
                quarter(0, True)
                with pe.Fori(1, 4) as c:
                    quarter(c, False)

            pe.wait_ge(vecs_loaded, 32)
            pe.wait_ge(tab_loaded, 48)
            for n, (a, b) in enumerate(TAB_CUTS):
                rows, r = (REL, rel) if b <= TAB1 else (REL2, rel2)
                nc.tensor.matmul(ps[0:HEADS, n, 0:b - a], r[:, :], buckets[0:rows, a:b], start=True, stop=True).then_inc(mt_full, 1)
            norm_sum(0)
            pe.wait_ge(mt_free, len(TAB_CUTS))
            with pe.Fori(0, 2) as i:
                for c in range(6):
                    unit("conv_in", c, H1, turn=i * 6, ready=(lambda k: (h_ready, k + 1)) if not c else None,
                         free=None if c else i * 10 + T0["conv_in"])
            for c in range(4):
                unit("conv_out", c, G, ready=(lambda k: (g_ready, k + 1)) if not c else None)
            norm_sum(1)
            mlp("mlp0", 1)
            norm_sum(2)

            for c in range(6):
                unit("kv", c, H1, ready=(lambda k: (h_ready, KT * 2 + k + 1)) if not c else None)
                if c in (3, 5):
                    for m in range(2):
                        n = 2 * (c // 2 - 1) + m
                        pe.wait_ge(mt_free, T0["kv"] + 2 * c + m + 1)
                        if n >= 2:
                            pe.wait_ge(vt_free, n - 1)
                        for t in range(QT):
                            mm = nc.tensor.transpose(ps[:, 4 + m, t * P:(t + 1) * P], Vf[:, m, t * P:(t + 1) * P], ident)
                        mm.then_inc(vt_full, 1)

            for c in range(4):
                u = U0["phi"] + c
                pe.wait_ge(lo_done, u + 1)
                pe.wait_ge(mt_free, T0["phi"] + (c - 1 if c else -2))
                s, kv = u % 2, c // 2
                for k in range(16):
                    if c % 2 == 0:
                        pe.wait_ge(phi_ready, 16 * kv + k + 1)
                    at = slice(k * P, (k + 1) * P)
                    for j, (w, x) in enumerate(((whi, phi_hi), (whi, phi_lo), (wlo, phi_hi))):
                        mm = nc.tensor.matmul(ps[:, 2 * s, 0:GROUPS * N_CMP], w[:, s, at], x[:, kv, k, :],
                                              start=k + j == 0, stop=k == 15 and j == 2)
                mm.then_inc(mt_full, 1)
            unit("gate", 0, H1, m_tiles=1, turn_m=1, ready=lambda k: (h_ready, KT * 3 + k + 1))
            pe.wait_ge(ctab_loaded, 16 + 16 * QT * P // CMP_STRIDE)
            pe.wait_ge(hid_ready, 2 + 2 * QT)
            pe.wait_ge(vt_free, 4)
            for m in range(2):
                mm = nc.tensor.matmul(ps[:, 4, 0:GROUPS * CMP_PAD], w2[:, m, 0:P], hid[:, 0, m, :, :].rearrange("p g n -> p (g n)"), start=m == 0, stop=m == 1)
            mm.then_inc(cmp_full, 1)
            for g in range(GROUPS):
                for m in range(2):
                    blocks = hidv[:, m, g, :, :].rearrange("p t n -> p (t n)")
                    mm = nc.tensor.matmul(ps[:, 5, g * DH:(g + 1) * DH], blocks, w2[:, m, P:P + DH], start=m == 0, stop=m == 1)
            mm.then_inc(cmp_full, 1)
            pe.wait_ge(gate_sig, 1)
            for t in range(QT):
                mm = nc.tensor.transpose(ps[:, 7, t * 3 * HEADS:(t + 1) * 3 * HEADS], gf[0:3 * HEADS, t * P:(t + 1) * P], ident[0:3 * HEADS, 0:3 * HEADS])
            mm.then_inc(gate_full, 1)
            pe.wait_ge(gate_ready, 1)
            pe.wait_ge(cmp_ready, 2)

            with pe.Fori(0, GROUPS) as g:
                unit("qo", 0, H1, turn=g * 2, turn_m=5, free=g * 10 + T0["qo"])
                pe.wait_ge(staged, g + 1)
                pe.wait_ge(mt_free, g * 10 + (T0["qo"] + 2))
                heads = [(h // 2, h % 2 * DH) for h in range(HPG)]

                def scores(r):
                    j, a = heads[r // 2]
                    if r:
                        pe.wait_ge(ttr_done, g * 32 + 4 * r)
                    for t in range(QT):
                        bank, at = ((0, 0), (1, 0), (0, P), (2, 0))[t]
                        nc.tensor.matmul(ps[:, bank, at:at + (t + 1) * P], Qs[a:a + DH, j, t * P:(t + 1) * P],
                                         Ks[a:a + DH, r % 2, 0:(t + 1) * P], start=True, stop=True)

                def turn(r):
                    if r:
                        pe.wait_ge(pt_act, g * 8 + r)
                        pe.wait_ge(pt_dve, g * 16 + 2 * r)
                    for t in range(QT):
                        pe.wait_ge(p_ready, g * 32 + (4 * r + t + 1))
                        for k in range(t + 1):
                            bank, at = turn_at(t, k)
                            mm = nc.tensor.transpose(ps[:, bank, at:at + P], Sb[:, r % 2, first(t) + k * P:first(t) + (k + 1) * P], ident)
                    mm.then_inc(pt_full, 1)

                def values(r):
                    j, a = heads[r // 2]
                    pe.wait_ge(pt_act, g * 8 + (r + 1))
                    pe.wait_ge(pt_dve, g * 16 + 2 * (r + 1))
                    for k in range(QT):
                        w = SEQ - k * P
                        mm = nc.tensor.matmul(ps[a:a + DH, 6 + j, k * P:SEQ], Vs[:, r % 2, k, :], PT[:, KEYS_AT[k]:KEYS_AT[k] + w],
                                              start=False, stop=k == QT - 1, skip_group_check=True)
                    if r % 4 == 3:
                        mm.then_inc(o_full, 1)

                scores(0)
                for h, (j, a) in enumerate(heads):
                    for t in range(QT):
                        at = (j * QT + t) * CMP_PAD
                        mm = nc.tensor.matmul(ps[:, 3 + h % 2, at:at + CMP_PAD], Qs[a:a + DH, j, t * P:(t + 1) * P], kcs[a:a + DH, :], start=True, stop=True)
                mm.then_inc(cs_full, 1)
                scores(1)
                pe.wait_ge(pc_ready, g + 1)
                for h in range(HPG):
                    mm = nc.tensor.transpose(ps[:, 4, h * P:(h + 1) * P], Sc[:, h * QT:(h + 1) * QT, :].rearrange("p t n -> p (t n)"), ident)
                mm.then_inc(ctr_full, 1)
                pe.wait_ge(ptc_ready, g + 1)
                for h, (j, a) in enumerate(heads):
                    for t in range(QT):
                        nc.tensor.matmul(ps[a:a + DH, 6 + j, t * P:(t + 1) * P], vcs[:, t, :], PTc[:, h, :],
                                         start=t == 0, stop=False, skip_group_check=True)
                for r in range(8):
                    if r < 6:
                        scores(r + 2)
                    if r:
                        values(r - 1)
                    turn(r)
                values(7)
                pe.wait_ge(lo_done, g * 2 + (U0["qo"] + 2))
                pe.wait_ge(o_ready, g * 2 + 2)
                s = (U0["qo"] + 1) % 2
                for m in range(KT):
                    if m >= 4:
                        pe.wait_ge(mt_free, g * 10 + (T0["qo"] + 2 + m - 3))
                    for k in range(2):
                        at = slice((k * KT + m) * P, (k * KT + m + 1) * P)
                        for i, (w, x) in enumerate(((whi, Ohi), (whi, Olo), (wlo, Ohi))):
                            mm = nc.tensor.matmul(ps[:, m % 4, :], w[:, s, at], x[:, k, :], start=k + i == 0, stop=k == 1 and i == 2)
                    mm.then_inc(mt_full, 1)
            norm_sum(3)
            mlp("mlp1", 4)
            norm_sum(4)

            def norm_sum2(n):
                pe.wait_ge(sq_add, KT * n + KT)
                for h in range(2):
                    mm = nc.tensor.matmul(ps[:, SUMS + h, 0:HALF], ones, acc[:, h * HALF:(h + 1) * HALF], start=True, stop=True)
                mm.then_inc(ssum, 1)

            def tile2(layer, c, m, rhs, ks=range(KT), k_tiles=KT, m_tiles=2, turn=0, ready=None, free=None):
                s, t = (U0[layer] + c) % 2, c * m_tiles + m
                if ks[0] == 0:
                    if m == 0:
                        pe.wait_ge(lo_done, turn + (U0[layer] + c + 1))
                    pe.wait_ge(mt_free, turn * m_tiles + (T0[layer] + t - 1) if free is None else free)
                hi, lo = rhs
                for k in ks:
                    if ready:
                        pe.wait_ge(*ready(k))
                    at = slice((k * m_tiles + m) * P, (k * m_tiles + m + 1) * P)
                    for j, (w, x) in enumerate(((whi, hi), (whi, lo), (wlo, hi))):
                        for h in range(2):
                            mm = nc.tensor.matmul(ps[:, 2 * (t % 2) + h, 0:HALF], w[:, s, at], x[:, k, h * HALF:(h + 1) * HALF],
                                                  start=k + j == 0, stop=k == k_tiles - 1 and j == 2)
                if ks[-1] == k_tiles - 1:
                    mm.then_inc(mt_full, 1)

            H2, A2 = (Hhi, Hlo), (AThi, ATlo)
            norm_sum2(5)
            tile2("dt", 0, 0, H2, m_tiles=1, ready=lambda k: (h_ready, KT * 5 + k + 1), free=T0["dt"])
            pe.wait_ge(cs_new, 1)
            for kind in (DT, CS):
                for c, (at, w) in enumerate(CHUNKS):
                    mm = nc.tensor.transpose(ps[0:w, 4 + kind, c * SSD_HEADS:(c + 1) * SSD_HEADS], dts[:, kind, at:at + w], ident[0:SSD_HEADS, 0:SSD_HEADS])
            mm.then_inc(tok_full, 1)
            pe.wait_ge(tok_new, 1)
            for c, (at, w) in enumerate(CHUNKS):
                last = ident[0:w, w - 1:w].to_broadcast([w, P])
                mm = nc.tensor.matmul(ps[:, 6, c * SSD_HEADS:(c + 1) * SSD_HEADS], last, tok[0:w, CS, c, :], start=True, stop=True)
            mm.then_inc(cl_full, 1)

            with pe.Fori(0, 2) as i:
                def row_tile(r, ks, rhs=H2, ready=None):
                    tile2("half", r // 2, r % 2, rhs, ks, turn=i * 14, ready=ready, free=None if r else i * 28 + T0["half"])

                def turned(gg, c):
                    n, (at, w) = gg * NC + c, CHUNKS[c]
                    chunk = slice(at, at + w)
                    if c == 0:
                        pe.wait_ge(xs_ready, i * 12 + 6 * (gg + 1))
                    else:
                        pe.wait_ge(h_new, i * 8 + (4 * gg + c))
                    for j in range(SSD_HPG // 2):
                        nc.tensor.transpose(ps[0:w, 4, j * P:(j + 1) * P], Y[:, 4 * gg + j, chunk], ident)
                    if c < NC - 1:
                        nc.tensor.transpose(ps[0:w, 5, 0:P], BC[:, gg, 0, chunk], ident)
                    nc.tensor.matmul(ps[0:w, 5, P:P + w], BC[:, gg, 0, chunk], BC[:, gg, 1, chunk], start=True, stop=True).then_inc(a_full, 1)

                def scanned(gg, c):
                    n, (at, w) = gg * NC + c, CHUNKS[c]
                    pe.wait_ge(decayed, i * 10 + (n + 1))
                    if n:
                        pe.wait_ge(y_done, i * 10 + n)
                    for h in range(SSD_HPG):
                        a = h % 2 * DH
                        mm = nc.tensor.matmul(ps[a:a + DH, 6, h // 2 * P:h // 2 * P + w], xdt[0:w, h * DH:(h + 1) * DH], L[0:w, n % 2, h, 0:w], start=True, stop=True)
                    for j in range(SSD_HPG // 2 if c else 0):
                        mm = nc.tensor.matmul(ps[:, 7, j * P:(j + 1) * P], Hs[:, j * P:(j + 1) * P], BC[:, gg, 1, at:at + w], start=True, stop=True)
                    mm.then_inc(y_full, 1)
                    if c < NC - 1:
                        pe.wait_ge(xd_ready, i * 8 + (4 * gg + c + 1))
                        pe.wait_ge(btok_ready, i * 8 + (4 * gg + c + 1))
                        nc.tensor.matmul(ps[:, 4, :], Btok[0:w, :], xdd[0:w, :], start=True, stop=True).then_inc(st_full, 1)

                def group_sum(gg):
                    pe.wait_ge(z_add, i * 8 + 4 * (gg + 1))
                    for h in range(2):
                        mm = nc.tensor.matmul(ps[:, 4 + 2 * gg + h, 0:HALF], ones, Gv[:, gg, h * HALF:(h + 1) * HALF], start=True, stop=True)
                    mm.then_inc(gsum, 1)

                low, high, all_k = range(0, 4), range(4, KT), range(KT)
                for r in range(20):
                    if r in SCAN_AT:
                        turned(*SCAN_AT[r])
                        row_tile(r, low)
                        scanned(*SCAN_AT[r])
                        row_tile(r, high)
                    else:
                        row_tile(r, all_k)
                    if r == 18:
                        group_sum(0)
                YN = (YNhi, YNlo)
                normed = lambda k: (yn_ready, i * 8 + (k + 1))
                row_tile(20, low, YN, normed)
                group_sum(1)
                row_tile(21, low, YN)
                row_tile(20, high, YN, normed)
                row_tile(21, high, YN)
                for r in range(22, 28):
                    row_tile(r, all_k, YN)

            for m in range(2):
                tile2("kv2", 0, m, H2)
            pe.wait_ge(mt_free, T0["kv2"] + 2)
            for c, (at, w) in enumerate(CHUNKS):
                bank, col = (4, (c - 1) * P) if c else (5, 0)
                mm = nc.tensor.transpose(ps[0:w, bank, col:col + P], GA[:, 0, at:at + w], ident)
            mm.then_inc(v_full, 1)

            with pe.Fori(0, 2) as i:
                for p in range(4):
                    base = i * 40 + 10 * p

                    def row_tile(rr, ks):
                        tile2("pair", rr // 2, rr % 2, H2, ks, turn=i * 6)

                    def scores(n):
                        if n >= 2:
                            pe.wait_ge(ttr2, base + (n if n == 8 else n - 1))
                        if n == 8:
                            for h in range(2):
                                rows = slice(h * DH, (h + 1) * DH)
                                nc.tensor.matmul(ps[:, 4 + h, 0:ROW0], Q2[rows, p % 2, 0:P], Ks2[rows, 0:ROW0], start=True, stop=True)
                            return
                        h, c = n // 4, 1 + n % 4
                        rows, (at, w) = slice(h * DH, (h + 1) * DH), CHUNKS[c]
                        q = Q2[rows, p % 2, at:at + P]
                        if c == 1:
                            nc.tensor.matmul(ps[:, 4 + n % 2, 0:ROW1], q, Ks2[rows, 0:ROW1], start=True, stop=True)
                        else:
                            nc.tensor.matmul(ps[:, 4 + n % 2, 0:ROW0], q, Ks2[rows, 0:ROW0], start=True, stop=True)
                            nc.tensor.matmul(ps[:, 4 + n % 2, ROW0:ROW], q, Ks2[rows, 1 + at - P:1 + at + P], start=True, stop=True)

                    def turn(n, p=p):
                        done = 9 * p + n
                        pe.wait_ge(p2_ready, i * 36 + (done + 1))
                        if n:
                            pe.wait_ge(pt2_dve, i * 36 + done)
                        elif p:
                            pe.wait_ge(at_ready, i * 4 + p)
                        if n == 8:
                            for h in range(2):
                                mm = nc.tensor.transpose(ps[0:N_META, 6, h * P:(h + 1) * P], Pb0[:, h, 1:ROW0], ident)
                        else:
                            c, at = 1 + n % 4, ROW0
                            nc.tensor.transpose(ps[0:N_META, 6, 0:P], Pb[:, n % 2, 1:ROW0], ident)
                            for j in range(2):
                                if j or c > 1:
                                    mm = nc.tensor.transpose(ps[:, 6, (1 + j) * P:(2 + j) * P], Pb[:, n % 2, at:at + P], ident)
                                    at += P
                        mm.then_inc(pt2_full, 1)

                    def values(n, p=p):
                        pe.wait_ge(pt2_dve, i * 36 + (9 * p + n + 1))
                        if n == 8:
                            for h in range(2):
                                mm = nc.tensor.matmul(ps[h * DH:(h + 1) * DH, 6, 448:448 + N_META], Vs2[0:N_META, 0, :],
                                                      PT0[:, h * N_META:(h + 1) * N_META], start=True, stop=True)
                            mm.then_inc(o2_full, 1)
                            return
                        h, c = n // 4, 1 + n % 4
                        out = ps[h * DH:(h + 1) * DH, 7, (c - 1) * P:c * P]
                        nc.tensor.matmul(out, Vs2[0:N_META, 0, :], PTm[:, :], start=True, stop=False, skip_group_check=True)
                        if c > 1:
                            nc.tensor.matmul(out, Vs2[:, c - 1, :], PT2[:, 0:P], start=False, stop=False, skip_group_check=True)
                        nc.tensor.matmul(out, Vs2[:, c, :], PT2[:, P:2 * P], start=False, stop=True, skip_group_check=True)

                    row_tile(3 * p, low)
                    if p:
                        turn(8, p - 1)
                    row_tile(3 * p, high)
                    if p:
                        values(8, p - 1)
                    else:
                        pe.wait_ge(kv_staged, i + 1)
                    pe.wait_ge(mt_free, i * 12 + (T0["pair"] + 3 * p + 1))
                    scores(0)
                    scores(1)
                    row_tile(3 * p + 1, all_k)
                    for n in range(8):
                        if n < 7:
                            scores(n + 2)
                        if n:
                            values(n - 1)
                        turn(n)
                        row_tile(3 * p + 2, range(n, n + 1))
                    values(7)
                    if p == 3:
                        turn(8)
                        values(8)
            for c in range(4):
                for m in range(2):
                    tile2("att", c, m, A2, ready=(lambda k: (at_ready, k + 1)) if not c + m else None)
            for c in range(4):
                for m in range(2):
                    tile2("out", c, m, H2, ready=(lambda k: (mg_ready, k + 1)) if not c + m else None)
            norm_sum2(6)
            for f, (a, b) in enumerate(((0, FF_CUT), (FF_CUT, FFT))):
                def pair(c, turn, first):
                    for m in range(2):
                        tile2(f"ff_in{f}", c, m, A2, turn=turn, ready=(lambda k: (h_ready, KT * 6 + k + 1)) if first and not m else None)
                pair(0, 0, not f)
                pair(1, 0, False)
                with pe.Fori(1, (b - a) // 2) as i:
                    for c in range(2):
                        pair(c, i * 2, False)
                for c in range(KT):
                    tile2(f"ff_out{f}", c, 0, (Fhi, Flo), range(b - a), b - a, 1, ready=(lambda k: (f_ready, a + k + 1)) if not c else None)
            norm_sum2(7)

        @block.vector
        def _(dve):
            own = Link(dve, dve_own)

            def norm_tile(n, part, k, slot, gain, a=N_META, hi=Hhi, lo=Hlo):
                if gain:
                    dve.wait_ge(h_hi, k + (KT * part + 1))
                    nc.vector.scalar_tensor_tensor(lo[:, k, a:], X[:, k, a:], vec(gain, k), hi[:, k, a:].bitcast(F32),
                                                   ALU.mult, ALU.subtract).then_inc(h_ready, 1)
                dve.wait_ge(sq_done, k + (KT * n + 1))
                if n or k:
                    dve.wait_ge(sq_add, k + KT * n)
                nc.vector.tensor_tensor(acc[:, a:], acc[:, a:], sq[:, slot, a:], ALU.add).then_inc(sq_add, 1)

            def norm_scale(n, sums=ps[:, SUMS, :], a=N_META):
                v, r, t = acc[:, a:], R[:, a:], R2[:, a:]
                if len(sums.shape) == 3:
                    v, r, t = (z.rearrange("p (h n) -> p h n", h=2) for z in (v, r, t))
                dve.wait_ge(ssum, n + 1)
                nc.vector.tensor_scalar(v, sums, 1.0 / D, EPS, ALU.mult, ALU.add).then_inc(variance, 1)
                dve.wait_ge(rms, n + 1)
                own.mark(nc.vector.reciprocal(r, t))
                own.wait()
                own.mark(nc.vector.tensor_tensor(t, r, r, ALU.mult))
                own.wait()
                own.mark(nc.vector.tensor_tensor(t, t, v, ALU.mult))
                own.wait()
                own.mark(nc.vector.tensor_scalar(t, t, -0.5, 1.5, ALU.mult, ALU.add))
                own.wait()
                nc.vector.tensor_tensor(r, r, t, ALU.mult).then_inc(rstd, 1)
                own.mark(nc.vector.memset(acc[:, :], 0.0))
                dve.wait_ge(rstd, n + 1)
                own.wait()

            def mlp(layer, n, part, gain):
                base = 0 if layer == "mlp0" else MLP_TILES
                def quarter(c, last):
                    for j in range(4):
                        for m in range(2):
                            t = T0[layer] + 2 * j + m + 1
                            k = base + 2 * j + m + 1
                            dve.wait_ge(mt_full, c * 16 + t)
                            nc.vector.tensor_tensor(mt[:, m, :], ps[:, 2 * ((U0[layer] + j) % 2) + m, :], R1, ALU.mult).then_inc(mt_free, 1)
                            dve.wait_ge(mt_free, c * 16 + t)
                            nc.vector.scalar_tensor_tensor(mid[:, m, :], mt[:, m, :], 0.0, mt[:, m, :], ALU.max, ALU.mult).then_inc(m_new, 1)
                            dve.wait_ge(m_hi, c * KT + k)
                            nc.vector.tensor_tensor(Mlo[:, 2 * j + m, :], mid[:, m, :], Mhi[:, 2 * j + m, :].bitcast(F32),
                                                    ALU.subtract).then_inc(m_ready, 1)
                    for j in range(4):
                        for m in range(2):
                            t = T0[layer] + 8 + 2 * j + m + 1
                            dve.wait_ge(mt_full, c * 16 + t)
                            x = X[:, 2 * j + m, N_META:TOK]
                            nc.vector.tensor_tensor(x, x, ps[:, 2 * ((U0[layer] + j) % 2) + m, :], ALU.add).then_inc(mt_free, 1)
                            if last:
                                norm_tile(n, part, 2 * j + m, m, gain)
                with dve.Fori(0, 3) as c:
                    quarter(c, False)
                quarter(3, True)
                norm_scale(n)

            nc.vector.memset(vbuf[:, :, 0:2], 0.0).then_inc(dve_own, 1)
            own.n += 1
            own.mark(nc.vector.memset(acc[:, :], 0.0))
            own.wait()
            dve.wait_ge(vecs_loaded, 32)
            dve.wait_ge(x_loaded, 32)
            for n, (a, b) in enumerate(TAB_CUTS):
                dve.wait_ge(mt_full, n + 1)
                nc.vector.tensor_copy(table[:, a:b], ps[0:HEADS, n, 0:b - a]).then_inc(mt_free, 1)
            for k in range(KT):
                norm_tile(0, 0, k, k % 2, "norm_mix0")
            norm_scale(0)
            own.mark(nc.vector.tensor_tensor(R2[:, N_META:TOK], R1, R1, ALU.mult))
            own.wait()
            with own.loop(2, 16) as i:
                for c in range(6):
                    pair, what = c // 3, c % 3
                    for m in range(2):
                        t = i * 12 + (T0["conv_in"] + 2 * c + m + 1)
                        k = i * 4 + (2 * pair + m)
                        out = ps[:, 2 * ((U0["conv_in"] + c) % 2) + m, :]
                        dve.wait_ge(mt_full, t)
                        if what == 0:
                            nc.vector.tensor_tensor(ct[:, m, :], out, R2[:, N_META:TOK], ALU.mult).then_inc(mt_free, 1)
                        elif what == 1:
                            dve.wait_ge(mt_free, t - 2)
                            nc.vector.tensor_tensor(vbuf[:, m, 2:], out, ct[:, m, :], ALU.mult).then_inc(mt_free, 1)
                        else:
                            nc.vector.tensor_tensor(gt[:, m, :], out, R1, ALU.mult).then_inc(mt_free, 1)
                            dve.wait_ge(mt_free, t)
                            nc.vector.tensor_tensor(t_at(Ghi, k), gt[:, m, :], cv[:, m, :], ALU.mult).then_inc(g_hi, 1)
                            own.mark(nc.vector.tensor_tensor(gt[:, m, :], gt[:, m, :], cv[:, m, :], ALU.mult))
                            dve.wait_ge(g_hi, k + 1)
                            own.wait()
                            nc.vector.tensor_tensor(t_at(Glo, k), gt[:, m, :], t_at(Ghi, k).bitcast(F32), ALU.subtract).then_inc(g_ready, 1)
                    if what == 1:
                        dve.wait_ge(mt_free, i * 12 + (T0["conv_in"] + 2 * c + 2))
                        for tap in range(3):
                            marks = []
                            for m in range(2):
                                k = i * 4 + (2 * pair + m)
                                w = vec_at("conv_w", k + tap * KT)
                                v = vbuf[:, m, tap:tap + SEQ]
                                if tap == 0:
                                    own.mark(nc.vector.tensor_scalar(cv[:, m, :], v, w, None, ALU.mult))
                                else:
                                    own.wait(own.at() - 1)
                                    own.mark(nc.vector.scalar_tensor_tensor(cv[:, m, :], v, w, cv[:, m, :], ALU.mult, ALU.add))
                        own.wait()
            for c in range(4):
                for m in range(2):
                    k = 2 * c + m
                    dve.wait_ge(mt_full, T0["conv_out"] + k + 1)
                    x = X[:, k, N_META:TOK]
                    nc.vector.tensor_tensor(x, x, ps[:, 2 * ((U0["conv_out"] + c) % 2) + m, :], ALU.add).then_inc(mt_free, 1)
                    norm_tile(1, 1, k, m, "norm_mlp0")
            norm_scale(1)
            mlp("mlp0", 2, 2, "kv_norm")

            dve.wait_ge(tab_stored, 16)
            own.mark(nc.vector.memset(hid[:, :, :, :, :], 0.0))
            own.mark(nc.vector.memset(hidv[:, :, :, :, :], 0.0))
            for c in range(6):
                for m in range(2):
                    t = T0["kv"] + 2 * c + m + 1
                    out = ps[:, 2 * ((U0["kv"] + c) % 2) + m, :]
                    dve.wait_ge(mt_full, t)
                    if c in (3, 5):
                        if c == 5:
                            dve.wait_ge(vt_full, m + 1)
                        nc.vector.tensor_tensor(Vf[:, m, :], out, R1, ALU.mult).then_inc(mt_free, 1)
                        continue
                    for half in range(2):
                        rows = slice(half * DH, (half + 1) * DH)
                        if c < 2:
                            to = kcat[rows, c, 2 * m + half, 1 - half:1 - half + SEQ]
                        else:
                            to = Kd[rows, c // 2 - 1, 2 * m + half, :]
                        mul = nc.vector.tensor_tensor(to, out[rows, :], R1[rows, :], ALU.mult)
                    mul.then_inc(mt_free, 1)
                if c in (3, 5):
                    for m in range(2):
                        n = 2 * (c // 2 - 1) + m
                        dve.wait_ge(vt_full, n + 1)
                        nc.vector.tensor_copy(Vt[:, c // 2 - 1, :, m * P:(m + 1) * P], ps[:, 4 + m, :].rearrange("p (t f) -> p t f", t=QT)).then_inc(vt_free, 1)
                if c in (2, 3):
                    kv = c - 2
                    for k in range(16):
                        dve.wait_ge(phi_h, 16 * kv + k + 1)
                        hi, lo = (x[:, kv, k, :].rearrange("p (g n) -> p g n", g=GROUPS) for x in (phi_hi, phi_lo))
                        nc.vector.scalar_tensor_tensor(lo, block_rows(kv, k), vec(("pe_k", "pe_v")[kv], k), hi.bitcast(F32),
                                                       ALU.add, ALU.subtract).then_inc(phi_ready, 1)
            for k in range(KT):
                dve.wait_ge(h_hi, KT * 3 + k + 1)
                nc.vector.scalar_tensor_tensor(Hlo[:, k, N_META:TOK], X[:, k, N_META:TOK], vec("norm_mix1", k),
                                               Hhi[:, k, N_META:TOK].bitcast(F32), ALU.mult, ALU.subtract).then_inc(h_ready, 1)
            for c in range(4):
                dve.wait_ge(mt_full, T0["phi"] + c + 1)
                nc.vector.tensor_copy(hid[:, c // 2, c % 2, :, 0:N_CMP],
                                      ps[:, 2 * ((U0["phi"] + c) % 2), 0:GROUPS * N_CMP].rearrange("p (g n) -> p g n", g=GROUPS)).then_inc(mt_free, 1)
            dve.wait_ge(mt_full, T0["gate"] + 1)
            nc.vector.tensor_tensor(gf[0:3 * HEADS, :], ps[0:3 * HEADS, 2 * (U0["gate"] % 2), :], R1[0:3 * HEADS, :], ALU.mult).then_inc(mt_free, 1)
            dve.wait_ge(cmp_full, 1)
            nc.vector.tensor_copy(kcmp[:, :, :], ps[:, 4, 0:GROUPS * CMP_PAD].rearrange("p (g n) -> p g n", g=GROUPS)).then_inc(cmp_ready, 1)
            dve.wait_ge(cmp_full, 2)
            nc.vector.tensor_copy(vcmp[:, :, :], ps[:, 5, 0:GROUPS * DH].rearrange("p (g d) -> p g d", g=GROUPS)).then_inc(cmp_ready, 1)
            dve.wait_ge(gate_full, 1)
            own.mark(nc.vector.tensor_copy(gates[:, :, :], ps[:, 7, 0:QT * 3 * HEADS].rearrange("p (t c) -> p t c", t=QT)))
            own.wait()
            seen = gates[:, 0, 0:3 * HEADS:3]
            nc.vector.tensor_scalar(seen, seen, vec("has_any"), None, ALU.mult).then_inc(gate_ready, 1)
            dve.wait_ge(gate_ready, 1)
            dve.wait_ge(ctab_loaded, 16 + 16 * QT * P // CMP_STRIDE)

            with own.loop(GROUPS, 16) as g:
                for m in range(2):
                    dve.wait_ge(mt_full, g * 10 + (T0["qo"] + m + 1))
                    nc.vector.scalar_tensor_tensor(Qs[:, m, :], ps[:, 2 * (U0["qo"] % 2) + m, :], DH ** -0.5, R1, ALU.mult, ALU.mult).then_inc(mt_free, 1)

                def scores(r):
                    for t in range(QT):
                        bank, at = ((0, 0), (1, 0), (0, P), (2, 0))[t]
                        w = (t + 1) * P
                        nc.vector.tensor_tensor_reduce(Sb[:, r % 2, first(t):first(t) + w], ps[:, bank, at:at + w], near[:, r // 2, SEQ - w:SEQ],
                                                       -1.0, -2 * MASKED, ALU.add, ALU.min, nmax[:, r % 2, t:t + 1]).then_inc(ttr_done, 1)

                def coefs(r):
                    dve.wait_ge(exp_done, g * 32 + (4 * r + 4))
                    c = coef[:, r % 2, :]
                    own.mark(nc.vector.reciprocal(rsum[:, r % 2, :], rsum[:, r % 2, :]))
                    own.wait()
                    col = gates[:, :, bass.ds(g * (3 * HPG) + (3 * (r // 2) + 1 + r % 2), 1)].rearrange("p t c -> p (t c)")
                    nc.vector.tensor_tensor(c, rsum[:, r % 2, :], col, ALU.mult).then_inc(coef_ready, 1)

                def turned(r):
                    dve.wait_ge(pt_full, g * 8 + (r + 1))
                    nc.vector.tensor_copy(PT[:, SEQ:2 * SEQ], ps[:, 4, :]).then_inc(pt_dve, 1)
                    nc.vector.tensor_copy(PT[:, 2 * SEQ:SPAN], ps[:, 5, 0:2 * P]).then_inc(pt_dve, 1)

                def heads_out(j):
                    dve.wait_ge(o_hi, g * 2 + (j + 1))
                    nc.vector.tensor_tensor(Olo[:, j, :], ps[:, 6 + j, :], Ohi[:, j, :].bitcast(F32), ALU.subtract).then_inc(o_ready, 1)

                n = HPG * QT
                wide = [P, n, CMP_PAD]
                dve.wait_ge(near_loaded, g * 16 + 16)
                dve.wait_ge(cs_full, g + 1)
                own.mark(nc.vector.tensor_tensor(
                    Sc[:, :, :].rearrange("p (j b t) n -> p b j (t n)", j=2, b=2),
                    ps[:, 3:5, 0:2 * P].rearrange("p b (j c) -> p b j c", j=2),
                    ctab[:, bass.ds(g * HPG, HPG), :].rearrange("p (j b) c -> p b j c", j=2), ALU.add))
                own.wait()
                own.mark(nc.vector.tensor_reduce(cst[:, 0, :], Sc[:, :, :], AX.X, ALU.max))
                own.wait()
                nc.vector.tensor_tensor(Sc[:, :, :], Sc[:, :, :], cst[:, 0, :].unsqueeze(2).to_broadcast(wide), ALU.subtract).then_inc(c_new, 1)
                scores(0)
                dve.wait_ge(c_exp, g + 1)
                own.mark(nc.vector.tensor_reduce(cst[:, 1, :], Sc[:, :, :], AX.X, ALU.add))
                own.wait()
                own.mark(nc.vector.reciprocal(cst[:, 2, :], cst[:, 1, :]))
                for h in range(HPG):
                    own.wait()
                    c = cst[:, 2, h * QT:(h + 1) * QT]
                    col = gates[:, :, bass.ds(g * (3 * HPG) + 3 * h, 1)].rearrange("p t c -> p (t c)")
                    own.mark(nc.vector.tensor_tensor(c, c, col, ALU.mult))
                own.wait()
                nc.vector.tensor_tensor(Sc[:, :, :], Sc[:, :, :], cst[:, 2, :].unsqueeze(2).to_broadcast(wide), ALU.mult).then_inc(pc_ready, 1)
                dve.wait_ge(ctr_full, g + 1)
                nc.vector.tensor_copy(PTc[:, :, :], ps[:, 4, :].rearrange("p (h q) -> p h q", h=HPG)).then_inc(ptc_ready, 1)
                scores(1)
                for r in range(8):
                    coefs(r)
                    turned(r)
                    if r < 6:
                        scores(r + 2)
                    if r == 4:
                        heads_out(0)
                heads_out(1)
                for m in range(KT):
                    dve.wait_ge(mt_full, g * 10 + (T0["qo"] + 2 + m + 1))
                    x = X[:, m, N_META:TOK]
                    nc.vector.tensor_tensor(x, x, ps[:, m % 4, :], ALU.add).then_inc(mt_free, 1)
            for k in range(KT):
                norm_tile(3, 4, k, k % 2, "norm_mlp1")
            norm_scale(3)
            mlp("mlp1", 4, None, None)
            for k in range(KT):
                x = X[:, k, N_META:]
                nc.vector.scalar_tensor_tensor(x, x, vec("final0", k), R1, ALU.mult, ALU.mult).then_inc(x_new, 1)

            for k in range(KT):
                norm_tile(5, 5, k, k % 2, "norm_mix2", 0)
            norm_scale(5, SUMS2, 0)

            v, e, d, s, z, q = (dtw[:, n, :] for n in range(6))
            rows = slice(0, SSD_HEADS)
            own.mark(nc.vector.memset(tok[:, :, :, :], 0.0))
            dve.wait_ge(mt_full, T0["dt"] + 1)
            nc.vector.tensor_tensor(halves(v), product(0, rows), halves(R[rows, :]), ALU.mult).then_inc(mt_free, 1)
            dve.wait_ge(mt_free, T0["dt"] + 1)
            own.mark(nc.vector.tensor_scalar(v, v, vecs[rows, VEC["dt_bias"]:VEC["dt_bias"] + 1], None, ALU.add))
            own.wait()
            nc.vector.scalar_tensor_tensor(e, v, -1.0, v, ALU.mult, ALU.max).then_inc(dt_abs, 1)
            dve.wait_ge(dt_exp, 2)
            own.mark(nc.vector.tensor_scalar(d, e, 2.0, None, ALU.add))
            own.wait()
            own.mark(nc.vector.reciprocal(d, d))
            own.wait()
            own.mark(nc.vector.tensor_tensor(s, e, d, ALU.mult))
            own.wait()
            own.mark(nc.vector.tensor_tensor(z, s, s, ALU.mult))
            own.wait()
            own.mark(nc.vector.tensor_scalar(q, z, 1 / 15, None, ALU.mult))
            for odd in (13, 11, 9, 7, 5, 3):
                own.wait()
                own.mark(nc.vector.scalar_tensor_tensor(q, q, 1 / odd, z, ALU.add, ALU.mult))
            own.wait()
            own.mark(nc.vector.scalar_tensor_tensor(q, q, 1.0, s, ALU.add, ALU.mult))
            own.mark(nc.vector.tensor_scalar(e, v, 0.0, None, ALU.max))
            own.wait()
            own.mark(nc.vector.scalar_tensor_tensor(dts[:, DT, :], q, 2.0, e, ALU.mult, ALU.add))
            own.wait()
            own.mark(nc.vector.tensor_scalar(d, dts[:, DT, :], al[:, :], -1.0, ALU.mult, ALU.mult))
            own.wait()
            for at, w in CHUNKS:
                scan = nc.vector.tensor_tensor_scan(dts[:, CS, at:at + w], ones[rows, 0:w], d[:, at:at + w], 0.0, ALU.mult, ALU.add)
            scan.then_inc(cs_new, 1)
            dve.wait_ge(tok_full, 1)
            for kind in (DT, CS):
                nc.vector.tensor_copy(tok[:, kind, 1:, :], ps[:, 4 + kind, SSD_HEADS:NC * SSD_HEADS].rearrange("p (c h) -> p c h", c=NC - 1))
                copy = nc.vector.tensor_copy(tok[0:N_META, kind, 0, :], ps[0:N_META, 4 + kind, 0:SSD_HEADS])
            copy.then_inc(tok_new, 1)
            dve.wait_ge(cl_full, 1)
            dve.wait_ge(tok_new, 1)
            nc.vector.tensor_tensor(tok[:, DECAY, :, :], ps[:, 6, 0:NC * SSD_HEADS].rearrange("p (c h) -> p c h", c=NC), tok[:, CS, :, :],
                                    ALU.subtract).then_inc(tok_diff, 1)
            dve.wait_ge(tok_ready, 1)

            dve.wait_ge(cs_stored, 16)
            own.mark(nc.vector.memset(stg[:, :, 0:SSD_TAPS - 1], 0.0))
            own.mark(nc.vector.memset(YS[:, :, :], 0.0))
            one = ones[:, 0:1]
            with own.loop(2, 73) as i:
                own.wait()
                own.mark(nc.vector.tensor_scalar(hv[:, :], vecs[:, bass.ds(i * HV + VEC["half"], HV)], one, None, ALU.mult))
                nc.vector.tensor_scalar(tokh[:, :, :, :].rearrange("p k c h -> p (k c) h"),
                                        tok[:, :, :, :].rearrange("p k c h -> p (k c) h")[:, :, bass.ds(i * (SSD_HEADS // 2), SSD_HEADS // 2)],
                                        one, None, ALU.mult).then_inc(tokh_ready, 1)
                dve.wait_ge(tokh_ready, i + 1)
                own.wait()
                heads = lambda x, w: x[0:w, :].rearrange("p (h d) -> p h d", h=SSD_HPG)

                def evacuate(r):
                    dve.wait_ge(mt_full, i * 28 + (T0["half"] + r + 1))
                    nc.vector.tensor_tensor(halves(stg[:, r % 2, SSD_TAPS - 1:]), product(r % 2), halves(R[:, :]), ALU.mult).then_inc(mt_free, 1)

                def convolve(r):
                    dve.wait_ge(mt_free, i * 28 + (T0["half"] + r + 1))
                    to, x = conv_out(r), stg[:, r % 2, :]
                    own.mark(nc.vector.tensor_scalar(to, x[:, 3:3 + TOK], conv_vec(r, 3), conv_vec(r, 4), ALU.mult, ALU.add))
                    for tap in range(3):
                        own.wait()
                        last = nc.vector.scalar_tensor_tensor(to, x[:, tap:tap + TOK], conv_vec(r, tap), to, ALU.mult, ALU.add)
                        if tap < 2:
                            own.mark(last)
                    last.then_inc(xbc_new, 1)

                def turned(gg, c):
                    n, w = gg * NC + c, CHUNKS[c][1]
                    by_head = lambda kind: tokh[0:w, kind, c, gg * SSD_HPG:(gg + 1) * SSD_HPG].unsqueeze(2).to_broadcast([w, SSD_HPG, DH])
                    dve.wait_ge(a_full, i * 10 + (n + 1))
                    own.mark(nc.vector.tensor_tensor(heads(xdt, w), heads(ps[:, 4, :], w), by_head(DT), ALU.mult))
                    nc.vector.tensor_tensor(cbm[0:w, 0:w], ps[0:w, 5, P:P + w], causal[0:w, 0:w], ALU.mult).then_inc(cb_ready, 1)
                    dve.wait_ge(l_ready, i * 10 + (n + 1))
                    dve.wait_ge(cb_ready, i * 10 + (n + 1))
                    own.wait()
                    l = L[0:w, n % 2, :, 0:w]
                    nc.vector.tensor_tensor(l, l, cbm[0:w, 0:w].unsqueeze(1).to_broadcast([w, SSD_HPG, w]), ALU.mult).then_inc(decayed, 1)
                    if c < NC - 1:
                        nc.vector.tensor_tensor(heads(xdd, w), heads(xdt, w), by_head(DECAY), ALU.mult).then_inc(xd_ready, 1)

                def scanned(gg, c):
                    n, (at, w) = gg * NC + c, CHUNKS[c]
                    dve.wait_ge(y_full, i * 10 + (n + 1))
                    if c:
                        dve.wait_ge(ecs_ready, i * 8 + (4 * gg + c))
                        own.mark(nc.vector.tensor_tensor(yoff[:, :, :], ps[:, 7, :].rearrange("p (j n) -> p j n", j=SSD_HPG // 2), ecs[:, n % 2, :, :], ALU.mult))
                    for j in range(SSD_HPG // 2):
                        y = Y[:, 4 * gg + j, at:at + w]
                        last = nc.vector.scalar_tensor_tensor(y, y, skip_vec(4 * gg + j), ps[:, 6, j * P:j * P + w], ALU.mult, ALU.add)
                    if c:
                        own.mark(last)
                        own.wait()
                        y = Y[:, 4 * gg:4 * gg + 4, at:at + w]
                        last = nc.vector.tensor_tensor(y, y, yoff[:, :, :], ALU.add)
                    last.then_inc(y_done, 1)
                    if c == NC - 1:
                        return
                    dve.wait_ge(st_full, i * 8 + (4 * gg + c + 1))
                    if c == 0:
                        nc.vector.tensor_copy(Hs[:, :], ps[:, 4, :]).then_inc(h_new, 1)
                    else:
                        dve.wait_ge(hd_ready, i * 6 + (3 * gg + c))
                        nc.vector.tensor_tensor(Hs[:, :], Hd[:, :], ps[:, 4, :], ALU.add).then_inc(h_new, 1)

                def gated(q):
                    dve.wait_ge(z_silu, i * 8 + (q + 1))
                    if q % 4 == 0:
                        dve.wait_ge(y_done, i * 10 + 5 * (q // 4 + 1))
                    nc.vector.tensor_tensor(Y[:, q, :], Y[:, q, :], stg[:, q % 2, SSD_TAPS - 1:], ALU.mult).then_inc(z_new, 1)

                def add_square(q):
                    dve.wait_ge(z_sq, i * 8 + (q + 1))
                    g = Gv[:, q // 4, :]
                    if q % 4:
                        dve.wait_ge(z_add, i * 8 + q)
                        nc.vector.tensor_tensor(g, g, sq[:, q % 2, :], ALU.add).then_inc(z_add, 1)
                    else:
                        nc.vector.tensor_copy(g, sq[:, q % 2, :]).then_inc(z_add, 1)

                def group_variance(gg):
                    dve.wait_ge(gsum, i * 2 + (gg + 1))
                    bank = 4 + 2 * gg
                    nc.vector.tensor_scalar(halves(Gv[:, gg, :]), ps[:, bank:bank + 2, 0:HALF], SSD_GROUPS / SSD_INNER, EPS, ALU.mult, ALU.add).then_inc(gvar, 1)

                def group_norm(gg):
                    v, r, t = Gv[:, gg, :], Gr[:, :], R2[:, :]
                    dve.wait_ge(gsqrt, i * 2 + (gg + 1))
                    own.mark(nc.vector.reciprocal(r, t))
                    own.wait()
                    own.mark(nc.vector.tensor_tensor(t, r, r, ALU.mult))
                    own.wait()
                    own.mark(nc.vector.tensor_tensor(t, t, v, ALU.mult))
                    own.wait()
                    own.mark(nc.vector.tensor_scalar(t, t, -0.5, 1.5, ALU.mult, ALU.add))
                    own.wait()
                    own.mark(nc.vector.tensor_tensor(r, r, t, ALU.mult))
                    own.wait()
                    for q in range(4 * gg, 4 * gg + 4):
                        nc.vector.scalar_tensor_tensor(Y[:, q, :], Y[:, q, :], gain_vec(q), r, ALU.mult, ALU.mult).then_inc(yn_new, 1)
                    for q in range(4 * gg, 4 * gg + 4):
                        dve.wait_ge(yn_new, i * 8 + (q + 1))
                        dve.wait_ge(yn_hi, i * 8 + (q + 1))
                        nc.vector.tensor_tensor(YNlo[:, q, :], Y[:, q, :], YNhi[:, q, :].bitcast(F32), ALU.subtract).then_inc(yn_ready, 1)

                for r in range(21):
                    if r:
                        evacuate(r - 1)
                    if r >= 14:
                        add_square(r - 14)
                    if r == 19:
                        group_variance(0)
                    if r in SCAN_AT:
                        turned(*SCAN_AT[r])
                    if 0 < r <= 12:
                        convolve(r - 1)
                    if r in SCAN_AT:
                        scanned(*SCAN_AT[r])
                    if r > 12:
                        gated(r - 13)
                    if r == 19:
                        group_norm(0)
                add_square(7)
                group_variance(1)
                group_norm(1)
                for r in range(20, 28):
                    dve.wait_ge(mt_full, i * 28 + (T0["half"] + r + 1))
                    y = halves(YS[:, r - 20, :])
                    nc.vector.tensor_tensor(y, y, product(r % 2), ALU.add).then_inc(mt_free, 1)

            own.mark(nc.vector.memset(Kd2[:, :, 0:1], 0.0))
            own.mark(nc.vector.memset(Vt2[:, 0, :], 0.0))
            own.mark(nc.vector.memset(Pb0[:, :, :], 0.0))
            dve.wait_ge(mt_full, T0["kv2"] + 1)
            for h in range(KV2):
                rows = slice(h * DH, (h + 1) * DH)
                mul = nc.vector.tensor_tensor(halves(Kd2[rows, h, 1:]), product(0, rows), halves(R[rows, :]), ALU.mult)
            mul.then_inc(mt_free, 1)
            dve.wait_ge(mt_full, T0["kv2"] + 2)
            nc.vector.tensor_tensor(halves(GA[:, 0, :]), product(1), halves(R[:, :]), ALU.mult).then_inc(mt_free, 1)
            dve.wait_ge(v_full, 1)
            own.wait()
            own.mark(nc.vector.tensor_copy(Vt2[:, 1:, :], ps[:, 4, :].rearrange("p (c d) -> p c d", c=NC - 1)))
            own.mark(nc.vector.tensor_copy(Vt2[0:N_META, 0, :], ps[0:N_META, 5, 0:P]))
            dve.wait_ge(kdup, 32)
            own.wait()
            with own.loop(2, 49) as i:
                own.mark(nc.vector.tensor_scalar(Ks2[:, :], t_at(Kd2, i), one, None, ALU.mult))
                nc.vector.tensor_scalar(Vs2[:, :, :], Vt2[:, :, bass.ds(i * DH, DH)], one, None, ALU.mult).then_inc(kv_staged, 1)
                for p in range(4):
                    base = i * 40 + 10 * p

                    def softmax_in(n):
                        if n == 8:
                            for h in range(2):
                                nc.vector.tensor_tensor_reduce(Pb0[0:N_META, h, :], ps[0:N_META, 4 + h, 0:ROW0], tab0[:, h, :], -1.0, -2 * MASKED,
                                                               ALU.add, ALU.min, nmax2[0:N_META, 2 + h:3 + h]).then_inc(ttr2, 1)
                            return
                        a, b = (0, ROW) if n % 4 else (ROW, ROW + ROW1)
                        nc.vector.tensor_tensor_reduce(Pb[:, n % 2, 0:b - a], ps[:, 4 + n % 2, 0:b - a], tabs[:, n // 4, a:b], -1.0, -2 * MASKED,
                                                       ALU.add, ALU.min, nmax2[:, n % 2:n % 2 + 1]).then_inc(ttr2, 1)

                    def softmax_out(n):
                        dve.wait_ge(exp2, base + (n + 1 if n < 8 else 10))
                        if n == 8:
                            own.mark(nc.vector.reciprocal(rsum2[0:N_META, 2:4], rsum2[0:N_META, 2:4]))
                            own.wait()
                            scale = rsum2[0:N_META, 2:4].unsqueeze(2).to_broadcast([N_META, 2, ROW0])
                            nc.vector.tensor_tensor(Pb0[0:N_META, :, :], Pb0[0:N_META, :, :], scale, ALU.mult).then_inc(p2_ready, 1)
                            return
                        c = rsum2[:, n % 2:n % 2 + 1]
                        own.mark(nc.vector.reciprocal(c, c))
                        own.wait()
                        row = Pb[:, n % 2, 0:ROW if n % 4 else ROW1]
                        nc.vector.tensor_scalar(row, row, c, None, ALU.mult).then_inc(p2_ready, 1)

                    def turned(n):
                        dve.wait_ge(pt2_full, i * 36 + (9 * p + n + 1))
                        if n == 8:
                            both = ps[0:N_META, 6, 0:2 * P].rearrange("p (h q) -> p h q", h=2)[:, :, 0:N_META]
                            copy = nc.vector.tensor_copy(PT0[:, :].rearrange("p (h q) -> p h q", h=2), both)
                        else:
                            nc.vector.tensor_copy(PTm[:, :], ps[0:N_META, 6, 0:P])
                            a = 0 if n % 4 else P
                            copy = nc.vector.tensor_copy(PT2[:, a:], ps[:, 6, P + a:3 * P])
                        copy.then_inc(pt2_dve, 1)

                    def heads_out(pp):
                        k = i * 4 + pp
                        dve.wait_ge(o2_full, k + 1)
                        own.mark(nc.vector.tensor_scalar(t_at(AThi, k, N_META), ps[:, 7, :], one, None, ALU.mult))
                        own.mark(nc.vector.tensor_scalar(t_at(AThi, k, 0, N_META), ps[:, 6, 448:448 + N_META], one, None, ALU.mult))
                        own.wait()
                        nc.vector.tensor_tensor(t_at(ATlo, k, N_META), ps[:, 7, :], t_at(AThi, k, N_META).bitcast(F32), ALU.subtract)
                        nc.vector.tensor_tensor(t_at(ATlo, k, 0, N_META), ps[:, 6, 448:448 + N_META], t_at(AThi, k, 0, N_META).bitcast(F32),
                                                ALU.subtract).then_inc(at_ready, 1)

                    def product_ready(rr):
                        t = i * 12 + (T0["pair"] + rr + 1)
                        dve.wait_ge(mt_full, t)
                        return t, product(rr % 2)

                    t, q = product_ready(3 * p)
                    nc.vector.scalar_tensor_tensor(halves(Q2[:, p % 2, :]), q, DH ** -0.5, halves(R[:, :]), ALU.mult, ALU.mult).then_inc(mt_free, 1)
                    if p:
                        heads_out(p - 1)
                    dve.wait_ge(tabs_loaded, i * 128 + 32 * (p + 1))
                    t, gate = product_ready(3 * p + 1)
                    nc.vector.tensor_tensor(halves(sq[:, 0, :]), gate, halves(R[:, :]), ALU.mult).then_inc(mt_free, 1)
                    softmax_in(0)
                    softmax_in(1)
                    dve.wait_ge(mt_free, t)
                    nc.vector.tensor_scalar(sq[:, 0, :], sq[:, 0, :], vec_at("gate_b", i * 4 + p), None, ALU.add).then_inc(gs_new, 1)
                    for n in range(8):
                        softmax_out(n)
                        turned(n)
                        if n < 7:
                            softmax_in(n + 2)
                        if n == 1:
                            dve.wait_ge(gs_sig, i * 4 + (p + 1))
                            own.mark(nc.vector.tensor_tensor(t_at(YS, i * 4 + p), t_at(YS, i * 4 + p), sq[:, 0, :], ALU.mult))
                    t, gate = product_ready(3 * p + 2)
                    nc.vector.tensor_tensor(halves_at(GA, i * 4 + p), gate, halves(R[:, :]), ALU.mult).then_inc(mt_free, 1)
                    dve.wait_ge(mt_free, t)
                    nc.vector.tensor_scalar(t_at(GA, i * 4 + p), t_at(GA, i * 4 + p), vec_at("gate_b", i * 4 + (KT + p)), None, ALU.add).then_inc(ga_new, 1)
                    softmax_out(8)
                    turned(8)
                heads_out(3)

            own.wait()
            for k in range(KT):
                dve.wait_ge(mt_full, T0["att"] + k + 1)
                if k == 0:
                    dve.wait_ge(ga_sig, KT)
                m = sq[:, k % 2, :]
                if k >= 2:
                    dve.wait_ge(mg_ready, k - 1)
                nc.vector.tensor_tensor(halves(m), product(k % 2), halves(GA[:, k, :]), ALU.mult).then_inc(mt_free, 1)
                dve.wait_ge(mt_free, T0["att"] + k + 1)
                nc.vector.tensor_tensor(m, m, YS[:, k, :], ALU.add).then_inc(mg_new, 1)
                dve.wait_ge(mg_hi, k + 1)
                nc.vector.tensor_tensor(Hlo[:, k, :], m, Hhi[:, k, :].bitcast(F32), ALU.subtract).then_inc(mg_ready, 1)
            for k in range(KT):
                dve.wait_ge(mt_full, T0["out"] + k + 1)
                x = halves(X[:, k, :])
                nc.vector.tensor_tensor(x, x, product(k % 2), ALU.add).then_inc(mt_free, 1)
                norm_tile(6, 6, k, k % 2, "norm_ffn", 0, AThi, ATlo)
            own.mark(nc.vector.memset(Fstg[:, :, 0:2], 0.0))
            norm_scale(6, SUMS2, 0)

            for f, (a, b) in enumerate(((0, FF_CUT), (FF_CUT, FFT))):
                with own.loop((b - a) // 2, 12) as i:
                    for c in range(2):
                        k = i * 2 + c
                        t = i * 4 + (T0[f"ff_in{f}"] + 2 * c + 1)
                        for m in range(2):
                            dve.wait_ge(mt_full, t + m)
                            nc.vector.tensor_tensor(halves(Fstg[:, m, 2:]), product(m), halves(R[:, :]), ALU.mult).then_inc(mt_free, 1)
                        for m in (1, 0):
                            taps = [vec_at("fconv", k * 8 + (8 * a + 4 * m + tap)) for tap in range(4)]
                            x, to = Fstg[:, m, :], Fcv[:, m, :]
                            dve.wait_ge(mt_free, t + m)
                            own.mark(nc.vector.tensor_scalar(to, x[:, 2:], taps[2], taps[3], ALU.mult, ALU.add))
                            own.wait()
                            own.mark(nc.vector.scalar_tensor_tensor(to, x[:, 0:TOK], taps[0], to, ALU.mult, ALU.add))
                            own.wait()
                            last = nc.vector.scalar_tensor_tensor(to, x[:, 1:1 + TOK], taps[1], to, ALU.mult, ALU.add)
                            if m:
                                last.then_inc(f_new, 1)
                            else:
                                own.mark(last)
                        own.wait()
                        dve.wait_ge(f_silu, k + (a + 1))
                        up, gate = Fcv[:, 0, :], Fcv[:, 1, :]
                        nc.vector.tensor_tensor(t_at(Fhi, k), up, gate, ALU.mult).then_inc(f_hi, 1)
                        own.mark(nc.vector.tensor_tensor(up, up, gate, ALU.mult))
                        dve.wait_ge(f_hi, k + (a + 1))
                        own.wait()
                        nc.vector.tensor_tensor(t_at(Flo, k), up, t_at(Fhi, k).bitcast(F32), ALU.subtract).then_inc(f_ready, 1)
                for k in range(KT):
                    dve.wait_ge(mt_full, T0[f"ff_out{f}"] + k + 1)
                    x = halves(X[:, k, :])
                    nc.vector.tensor_tensor(x, x, product(k % 2), ALU.add).then_inc(mt_free, 1)
                    if f:
                        norm_tile(7, None, k, k % 2, None, 0)
            norm_scale(7, SUMS2, 0)
            for k in range(KT):
                x = X[:, k, N_META:]
                nc.vector.scalar_tensor_tensor(x, x, vec("final2", k), R1, ALU.mult, ALU.mult).then_inc(out_new, 1)

def tiles_of(a):
    return np.ascontiguousarray(a.reshape(-1, P, a.shape[-1]).transpose(1, 0, 2))


def columns(w, *starts, width=2 * P):
    out = []
    for s in starts:
        cols = np.concatenate([w[:, a:a + P] for a in s], 1) if isinstance(s, tuple) else w[:, s:s + width]
        out.append(tiles_of(cols).reshape(P, -1))
    return out


def padded(u):
    return np.concatenate([u, np.zeros((P, UCOLS - u.shape[1]), u.dtype)], 1)


def bucket_of(dist):
    d = np.maximum(dist, 0)
    half = BUCKETS // 2
    far = half + (np.log(np.maximum(d, 1).astype(np.float32) / half) / math.log(MAX_DIST / half) * (BUCKETS - half)).astype(np.int32)
    return np.where(dist < 0, BUCKETS, np.where(d < half, d, np.minimum(far, BUCKETS - 1)))


def one_hot(dist, less_far=False):
    hot = (np.arange(REL)[:, None] == bucket_of(dist)[None, :]).astype(np.float32)
    if less_far:
        hot[BUCKETS - 1] -= (dist >= 0)
    return hot


def lay_out(a):
    n = {k: np.asarray(v) for k, v in a.items()}
    units = []
    w = n["a_w_in"][0]
    for j in range(4):
        units += columns(w, D + 256 * j, 2 * D + 256 * j, 256 * j)
    units += columns(n["a_w_out"][0], *range(0, D, 256))

    def mlp(layer):
        w1, w2 = n["mlp_w1"][layer], n["mlp_w2"][layer]
        out = []
        for c in range(4):
            out += columns(w1, *range(c * D, (c + 1) * D, 256))
            out += columns(w2[c * D:(c + 1) * D], *range(0, D, 256))
        return out
    units += mlp(0)
    units += columns(n["w_kv"], *range(0, 6 * GROUPS * DH, 256))
    for w in ("phi_k_w1", "phi_v_w1"):
        for m in range(PHI // P):
            units.append(tiles_of(n[w][:, m * P:(m + 1) * P]).reshape(P, -1))
    w, wo = n["b_w_qg"][0], n["b_w_o"][0]
    tail = np.zeros((D, P), np.float32)
    tail[:, :3 * HEADS] = w[:, HEADS * DH:]
    units.append(padded(tiles_of(tail).reshape(P, -1)))
    for g in range(GROUPS):
        units += columns(w, 256 * g)
        units.append(tiles_of(wo[256 * g:256 * (g + 1)]).reshape(P, -1))
    units += mlp(1)
    w = n["w_in_2"][0]
    z, xs, bm, cm, dt, q, kk, gs, ga = np.cumsum([0, SSD_INNER, SSD_INNER, SSD_GROUPS * STATE, SSD_GROUPS * STATE, SSD_HEADS, D, KV2 * DH * 2, D])
    tail = np.zeros((D, P), np.float32)
    tail[:, :SSD_HEADS] = w[:, dt:q]
    units.append(padded(tiles_of(tail).reshape(P, -1)))
    w_ssd = n["w_ssd_branch_2"][0]
    for i in range(2):
        for g in (2 * i, 2 * i + 1):
            units += columns(w, (bm + P * g, cm + P * g), xs + 512 * g, xs + 512 * g + 256)
        units += columns(w, *range(z + D * i, z + D * i + D, 256))
        units += columns(w_ssd[D * i:D * i + D], *range(0, D, 256))
    units += columns(w, kk)
    order = [a + P * j for j in range(KT) for a in (q, gs, ga)]
    units += columns(w, *zip(order[::2], order[1::2]))
    units += columns(n["w_attn_branch_2"][0], *range(0, D, 256))
    units += columns(n["w_out_2"][0], *range(0, D, 256))
    w, wo = n["w_ffn_in_2"][0], n["w_ffn_out_2"][0]
    for a, b in ((0, FF_CUT), (FF_CUT, FFT)):
        units += columns(w, *((P * c, DFF2 + P * c) for c in range(a, b)))
        for m in range(KT):
            units.append(padded(tiles_of(wo[a * P:b * P, m * P:(m + 1) * P]).reshape(P, -1)))
    assert len(units) == NU
    stream = np.stack(units)

    vecs = np.zeros((P, NVEC), np.float32)

    def put(name, v):
        v = np.asarray(v).reshape(-1, P).T
        vecs[:, VEC[name]:VEC[name] + v.shape[1]] = v
    for i in range(2):
        put(f"norm_mix{i}", n["norm_mix"][i])
        put(f"norm_mlp{i}", n["norm_mlp"][i])
    put("kv_norm", n["kv_norm"])
    put("final0", n["final_norm"])
    put("norm_mix2", n["norm_mix_w_2"][0])
    put("norm_ffn", n["norm_ffn_w_2"][0])
    put("final2", n["norm_final_w_2"])
    put("gate_b", n["gate_b_2"][0])
    vecs[:SSD_HEADS, VEC["dt_bias"]] = n["ssd_dt_bias_2"][0]
    vecs[:SSD_HEADS, VEC["a_log"]] = n["ssd_a_log_2"][0]
    taps = np.concatenate([n["ssd_conv_w_2"][0], n["ssd_conv_b_2"]]).reshape(SSD_TAPS + 1, -1, P)
    skip = np.repeat(n["ssd_d_2"][0], DH).reshape(-1, P)
    half = []
    for g in range(SSD_GROUPS):
        for t in (16 + g, 20 + g, 4 * g, 4 * g + 1, 4 * g + 2, 4 * g + 3):
            half += list(taps[:, t])
        if g % 2:
            half += list(skip[4 * g - 4:4 * g + 4]) + list(n["ssd_norm_w_2"][0].reshape(-1, P)[4 * g - 4:4 * g + 4])
    put("half", np.stack(half))
    taps = np.concatenate([n["ffn_conv_w_2"][0], n["ffn_conv_b_2"]]).reshape(4, 2, FFT, P)
    put("fconv", taps.transpose(2, 1, 0, 3))
    put("conv_w", n["a_conv_w"][0])
    vecs[:, VEC["eps"]] = EPS
    for k, name in enumerate(("cmp_pe_k", "cmp_pe_v")):
        put(("pe_k", "pe_v")[k], n[name].reshape(-1))
    vecs[:, VEC["quarter"]:VEC["quarter"] + QT] = np.arange(P)[:, None] // CMP_PAD == np.arange(QT)[None, :]
    vecs[:, VEC["has_any"]] = np.arange(P) >= CMP_BLOCK - 1
    rel = np.concatenate([n["rel_bias"], np.full((1, HEADS), MASKED, np.float32)])
    steps = np.arange(CMP_LEN) - (SEQ // CMP_STRIDE - 1)
    cmp_dist = np.arange(CMP_STRIDE)[:, None] - CMP_STRIDE * steps[None, :] - (CMP_BLOCK - 1)
    buckets = np.concatenate([one_hot(SEQ - 1 - np.arange(BAND_LEN), True), one_hot(cmp_dist.reshape(-1))], 1)
    band = 2 * P - 1 - np.arange(3 * P - 1)
    band = np.where(band < WINDOW2, band, -1)
    near = [2 * P] * N_META, band, P + N_META - 1 - np.arange(P + N_META - 1), N_META - 1 - np.arange(2 * N_META - 1)
    hot2 = np.concatenate([np.zeros((REL, 1), np.float32)] + [one_hot(np.asarray(d)) for d in near], 1)
    hot2 = np.concatenate([hot2, (np.arange(TAB2) == 0).astype(np.float32)[None]], 0)
    buckets = np.concatenate([np.pad(buckets, ((0, 1), (0, 0))), hot2], 1).astype(np.float32)
    rel2 = np.concatenate([n["rel_bias_2"], np.full((1, HEADS), MASKED, np.float32), n["attn_sinks_2"]])
    w2 = np.concatenate([tiles_of(n["phi_k_w2"]), tiles_of(n["phi_k_w2"]), tiles_of(n["phi_v_w2"])], 2)
    consts = np.stack([np.eye(P), np.ones((P, P)), np.triu(np.ones((P, P)))], 1).astype(np.float32)
    return {"x": tiles_of(n["x"][0].T), "stream": stream, "vecs": vecs, "consts": consts,
            "rel": rel, "rel2": rel2, "buckets": buckets, "phi_w2": w2, "meta": tiles_of(n["meta_tokens_2"].T)}



def kernel(**inputs):
    import concourse.bacc as bacc
    from concourse.bass_utils import run_bass_kernel_spmd

    arrays = lay_out(inputs)
    nc = bacc.Bacc("TRN2", target_bir_lowering=False, num_devices=1)
    io = {name: nc.dram_tensor(f"in_{name}", a.shape, F32, kind="ExternalInput").ap() for name, a in arrays.items()}
    io["out"] = nc.dram_tensor("out", (P, KT, SEQ), F32, kind="ExternalOutput").ap()
    program(nc, io)
    r = run_bass_kernel_spmd(nc, [{f"in_{name}": a for name, a in arrays.items()}], core_ids=[0])
    out = r.results[0]["out"]
    return np.ascontiguousarray(out.transpose(2, 1, 0).reshape(1, SEQ, D))
```
